# Optimizing a Trainium2 kernel written in Bass

```python
import math
import jax, jax.numpy as jnp
from jax import lax
import numpy as np

D_MODEL = 1024
BATCH = 1
SEQ = 256
DEPTH = 1
DEC_BATCH = 8
DEC_SEQ = 1
PAST_LEN = 256
PAGE_SIZE = 128

H_A = 4
DK_A = 128
DV_A = 128
W_A = H_A * DV_A
HGRN_CHUNK = 64
H_B = 4
DK_B = 64
DV_B = 2 * DK_B
QK_B = H_B * 2 * DK_B
W_B = H_B * DV_B
Q_BLOCK = 128
NEG_INF = -1e30
N_EXPERTS = 32
TOP_K = 4
D_FF = D_MODEL
SWIGLU_LIMIT = 7.0
SWIGLU_ALPHA = 1.702
MOE_BLOCK = 128
EPS = 1e-6
IN_SPLITS = (W_A, 2 * W_A, 3 * W_A, 4 * W_A, 4 * W_A + QK_B, 4 * W_A + 2 * QK_B,
             4 * W_A + 2 * QK_B + W_B, 4 * W_A + 2 * QK_B + W_B + D_MODEL)
D_IN = 4 * W_A + 2 * QK_B + W_B + 2 * D_MODEL

kernel_name = 'hgrn2_diffattn_moe_decoder_step'

def _rmsnorm(x, g):
    xf = x.astype(jnp.float32)
    y = xf * lax.rsqrt(jnp.mean(xf * xf, axis=-1, keepdims=True) + EPS)
    return (y * g.astype(jnp.float32)).astype(x.dtype)

def _modulation(c, w_mod, b_mod):
    m = jax.nn.silu(c) @ w_mod + b_mod
    return jnp.split(m[:, None, :], 6, axis=-1)

def _hgrn2(aq, af, ai, ag, s0, lb, g_norm):
    B, L, _ = aq.shape
    f32 = jnp.float32
    lb = lb.reshape(H_A, DK_A).astype(f32)
    q = aq.reshape(B, L, H_A, DK_A).astype(f32)
    f = lb + (1.0 - lb) * jax.nn.sigmoid(af.reshape(B, L, H_A, DK_A).astype(f32))
    k = 1.0 - f
    v = ai.reshape(B, L, H_A, DV_A).astype(f32)
    C = math.gcd(L, HGRN_CHUNK)
    NC = L // C
    q, k, v = (t.reshape(B, NC, C, H_A, t.shape[-1]) for t in (q, k, v))
    gc = jnp.cumsum(jnp.log(f).reshape(B, NC, C, H_A, DK_A), axis=2)
    q_dec = q * jnp.exp(gc)
    k_dec = k * jnp.exp(-gc)
    causal = jnp.tril(jnp.ones((C, C), dtype=bool))
    a = jnp.where(causal, jnp.einsum('bntha,bnsha->bnhts', q_dec, k_dec), 0.0)
    o_intra = jnp.einsum('bnhts,bnshv->bnthv', a, v)
    g_last = gc[:, :, -1]
    kv = jnp.einsum('bnsha,bnshv->bnhav', k * jnp.exp(g_last[:, :, None] - gc), v)

    def step(S, xs):
        qd, gl, kv_c = xs
        o = jnp.einsum('btha,bhav->bthv', qd, S)
        return jnp.exp(gl)[..., None] * S + kv_c, o

    s_fin, o_inter = lax.scan(step, s0.astype(f32),
                              (jnp.moveaxis(q_dec, 1, 0), jnp.moveaxis(g_last, 1, 0), jnp.moveaxis(kv, 1, 0)))
    o = (o_intra + jnp.moveaxis(o_inter, 0, 1)).reshape(B, L, H_A, DV_A)
    o = _rmsnorm(o, g_norm).reshape(B, L, W_A) * jax.nn.silu(ag.astype(f32))
    return o.astype(aq.dtype), s_fin

def _alibi_slopes():
    return jnp.exp2(-8.0 * jnp.arange(1, H_B + 1, dtype=jnp.float32) / H_B)

def _diff_scores(q, k, v, q_pos, k_pos, lam):
    s = jnp.einsum('bqhmd,bkhmd->bhmqk', q, k).astype(jnp.float32) * (DK_B ** -0.5)
    dist = (q_pos[:, None] - k_pos[None, :]).astype(jnp.float32)
    s = s - _alibi_slopes()[None, :, None, None, None] * dist
    s = jnp.where(dist >= 0, s, NEG_INF)
    p = jax.nn.softmax(s, axis=-1)
    p = p[:, :, 0] - lam * p[:, :, 1]
    return jnp.einsum('bhqk,bkhv->bqhv', p, v.astype(jnp.float32))

def _prompt_diff_attention(q, k, v, lam):
    B, L = q.shape[0], q.shape[1]
    nb = L // Q_BLOCK
    pos = jnp.arange(L, dtype=jnp.int32)
    kk = k.reshape(B, L, H_B, 2, DK_B)
    qb = jnp.moveaxis(q.reshape(B, nb, Q_BLOCK, H_B, 2, DK_B), 1, 0)
    pb = pos.reshape(nb, Q_BLOCK)
    ob = lax.map(lambda a: _diff_scores(a[0], kk, v, a[1], pos, lam), (qb, pb))
    return jnp.moveaxis(ob, 0, 1).reshape(B, L, H_B, DV_B)

def _clamped_swiglu(xb, wgu, bgu, wd, bd):
    gu = xb @ wgu + bgu
    glu, lin = gu[:, :D_FF], gu[:, D_FF:]
    glu = jnp.minimum(glu, SWIGLU_LIMIT)
    lin = jnp.clip(lin, -SWIGLU_LIMIT, SWIGLU_LIMIT)
    return ((lin + 1.0) * glu * jax.nn.sigmoid(SWIGLU_ALPHA * glu)) @ wd + bd

def _moe(h, w_router, b_router, w_gate_up, b_gate_up, w_down, b_down):
    B, L, D = h.shape
    T = B * L
    xt = h.reshape(T, D)
    logits = (xt @ w_router + b_router).astype(jnp.float32)
    top_val, top_idx = lax.top_k(logits, TOP_K)
    gates = jax.nn.softmax(top_val, axis=-1)
    n_assign = T * TOP_K
    e_flat = top_idx.reshape(-1)
    tok_flat = jnp.arange(n_assign, dtype=jnp.int32) // TOP_K
    order = jnp.argsort(e_flat)
    e_sorted = e_flat[order]
    tok_sorted = tok_flat[order]
    gate_sorted = gates.reshape(-1)[order]
    counts = jnp.bincount(e_flat, length=N_EXPERTS)
    padded = (counts + MOE_BLOCK - 1) // MOE_BLOCK * MOE_BLOCK
    pad_end = jnp.cumsum(padded)
    pad_start = pad_end - padded
    start = jnp.cumsum(counts) - counts
    dest = pad_start[e_sorted] + jnp.arange(n_assign, dtype=jnp.int32) - start[e_sorted]
    n_blocks = -(-n_assign // MOE_BLOCK) + N_EXPERTS
    x_buf = jnp.zeros((n_blocks * MOE_BLOCK, D), xt.dtype).at[dest].set(xt[tok_sorted])
    block_expert = jnp.minimum(
        jnp.searchsorted(pad_end, jnp.arange(n_blocks, dtype=pad_end.dtype) * MOE_BLOCK, side='right'),
        N_EXPERTS - 1)

    def expert_block(a):
        xb, e = a
        return _clamped_swiglu(xb, w_gate_up[e], b_gate_up[e], w_down[e], b_down[e])

    y_buf = lax.map(expert_block, (x_buf.reshape(n_blocks, MOE_BLOCK, D), block_expert)).reshape(-1, D)
    y = jax.ops.segment_sum(y_buf[dest] * gate_sorted[:, None].astype(y_buf.dtype), tok_sorted,
                            num_segments=T)
    return y.reshape(B, L, D).astype(h.dtype)

def _trunk_layer(x, c, s_hgrn0, k_cache, v_cache, page_table, l, lb,
                 w_mod, b_mod, g_pre_mix, g_post_mix, g_pre_ffn, g_post_ffn,
                 w_in, g_hgrn, lam_q1, lam_k1, lam_q2, lam_k2, g_subln,
                 w_proj_a, w_proj_b, w_out,
                 w_router, b_router, w_gate_up, b_gate_up, w_down, b_down):
    B, L, _ = x.shape
    sh1, sc1, gt1, sh2, sc2, gt2 = _modulation(c, w_mod, b_mod)
    h = _rmsnorm(x, g_pre_mix) * (1.0 + sc1) + sh1
    aq, af, ai, ag, bq, bk, bv, gate_a, gate_b = jnp.split(h @ w_in, IN_SPLITS, axis=-1)
    o_a, s_new = _hgrn2(aq, af, ai, ag, s_hgrn0, lb, g_hgrn)
    lam_init = 0.8 - 0.6 * math.exp(-0.3 * l)
    lam = (jnp.exp(jnp.sum(lam_q1.astype(jnp.float32) * lam_k1.astype(jnp.float32)))
           - jnp.exp(jnp.sum(lam_q2.astype(jnp.float32) * lam_k2.astype(jnp.float32))) + lam_init)
    q = bq.reshape(B, L, H_B, 2, DK_B)
    k_new = bk.reshape(B, L, H_B, 2 * DK_B)
    v_new = bv.reshape(B, L, H_B, DV_B)
    if k_cache is None:
        o_b = _prompt_diff_attention(q, k_new, v_new, lam)
    else:
        past = page_table.shape[1] * k_cache.shape[1]
        k_past = k_cache[page_table].reshape(B, past, H_B, 2 * DK_B)
        v_past = v_cache[page_table].reshape(B, past, H_B, DV_B)
        k_all = jnp.concatenate([k_past, k_new.astype(k_past.dtype)], axis=1)
        v_all = jnp.concatenate([v_past, v_new.astype(v_past.dtype)], axis=1)
        q_pos = past + jnp.arange(L, dtype=jnp.int32)
        k_pos = jnp.arange(past + L, dtype=jnp.int32)
        o_b = _diff_scores(q, k_all.reshape(B, past + L, H_B, 2, DK_B), v_all, q_pos, k_pos, lam)
    o_b = (_rmsnorm(o_b, g_subln) * (1.0 - lam_init)).reshape(B, L, W_B).astype(h.dtype)
    merged = jax.nn.sigmoid(gate_a) * (o_a @ w_proj_a) + jax.nn.sigmoid(gate_b) * (o_b @ w_proj_b)
    x = x + gt1 * _rmsnorm(merged @ w_out, g_post_mix)
    h2 = _rmsnorm(x, g_pre_ffn) * (1.0 + sc2) + sh2
    x = x + gt2 * _rmsnorm(_moe(h2, w_router, b_router, w_gate_up, b_gate_up, w_down, b_down), g_post_ffn)
    return x, s_new, k_new, v_new

def setup_inputs(seed: int = 0) -> dict:
    key = jax.random.key(seed)
    ks = jax.random.split(key, 32)
    f32 = jnp.float32
    n_pages = PAST_LEN // PAGE_SIZE
    n_used = DEC_BATCH * n_pages
    n_pool = n_used + max(1, n_used // 4)

    def nrm(k, shape, scale):
        return scale * jax.random.normal(k, shape, f32)

    def gain(k, shape):
        return 1.0 + 0.05 * jax.random.normal(k, shape, f32)

    page_table = jax.random.permutation(ks[5], n_pool)[:n_used].reshape(DEC_BATCH, n_pages).astype(jnp.int32)
    return {
        'x_prompt': nrm(ks[0], (BATCH, SEQ, D_MODEL), 1.0),
        'x_sample': nrm(ks[1], (DEC_BATCH, DEC_SEQ, D_MODEL), 1.0),
        'cache_k': nrm(ks[2], (DEPTH, n_pool, PAGE_SIZE, H_B, 2 * DK_B), 1.0),
        'cache_v': nrm(ks[3], (DEPTH, n_pool, PAGE_SIZE, H_B, DV_B), 1.0),
        'state_hgrn': nrm(ks[4], (DEPTH, DEC_BATCH, H_A, DK_A, DV_A), 0.5),
        'page_table': page_table,
        'c_prompt': nrm(ks[6], (BATCH, D_MODEL), 1.0),
        'c_sample': nrm(ks[7], (DEC_BATCH, D_MODEL), 1.0),
        'w_mod': nrm(ks[8], (DEPTH, D_MODEL, 6 * D_MODEL), 0.5 * D_MODEL ** -0.5),
        'b_mod': nrm(ks[9], (DEPTH, 6 * D_MODEL), 0.02),
        'g_pre_mix': gain(ks[10], (DEPTH, D_MODEL)),
        'g_post_mix': gain(ks[11], (DEPTH, D_MODEL)),
        'g_pre_ffn': gain(ks[12], (DEPTH, D_MODEL)),
        'g_post_ffn': gain(ks[13], (DEPTH, D_MODEL)),
        'w_in': nrm(ks[14], (DEPTH, D_MODEL, D_IN), D_MODEL ** -0.5),
        'hgrn_lb': nrm(ks[15], (DEPTH + 1, W_A), 0.1),
        'g_hgrn': gain(ks[16], (DEPTH, H_A, DV_A)),
        'lam_q1': nrm(ks[17], (DEPTH, DK_B), 0.1),
        'lam_k1': nrm(ks[18], (DEPTH, DK_B), 0.1),
        'lam_q2': nrm(ks[19], (DEPTH, DK_B), 0.1),
        'lam_k2': nrm(ks[20], (DEPTH, DK_B), 0.1),
        'g_subln': gain(ks[21], (DEPTH, DV_B)),
        'w_proj_a': nrm(ks[22], (DEPTH, W_A, D_MODEL), W_A ** -0.5),
        'w_proj_b': nrm(ks[23], (DEPTH, W_B, D_MODEL), W_B ** -0.5),
        'w_out': nrm(ks[24], (DEPTH, D_MODEL, D_MODEL), D_MODEL ** -0.5),
        'w_router': nrm(ks[25], (DEPTH, D_MODEL, N_EXPERTS), D_MODEL ** -0.5),
        'b_router': nrm(ks[26], (DEPTH, N_EXPERTS), 0.01),
        'w_gate_up': nrm(ks[27], (DEPTH, N_EXPERTS, D_MODEL, 2 * D_FF), D_MODEL ** -0.5),
        'b_gate_up': nrm(ks[28], (DEPTH, N_EXPERTS, 2 * D_FF), 0.01),
        'w_down': nrm(ks[29], (DEPTH, N_EXPERTS, D_FF, D_MODEL), D_FF ** -0.5),
        'b_down': nrm(ks[30], (DEPTH, N_EXPERTS, D_MODEL), 0.01),
    }

def reference(x_prompt, x_sample, cache_k, cache_v, state_hgrn, page_table, c_prompt, c_sample,
              w_mod, b_mod, g_pre_mix, g_post_mix, g_pre_ffn, g_post_ffn, w_in, hgrn_lb, g_hgrn,
              lam_q1, lam_k1, lam_q2, lam_k2, g_subln, w_proj_a, w_proj_b, w_out,
              w_router, b_router, w_gate_up, b_gate_up, w_down, b_down):
    lb_all = jnp.cumsum(jax.nn.softmax(hgrn_lb.astype(jnp.float32), axis=0), axis=0)
    y_p, y_s = x_prompt, x_sample
    k_p_list, v_p_list, s_p_list, k_s_list, v_s_list, s_s_list = [], [], [], [], [], []
    for l in range(DEPTH):
        wl = (w_mod[l], b_mod[l], g_pre_mix[l], g_post_mix[l], g_pre_ffn[l], g_post_ffn[l],
              w_in[l], g_hgrn[l], lam_q1[l], lam_k1[l], lam_q2[l], lam_k2[l], g_subln[l],
              w_proj_a[l], w_proj_b[l], w_out[l],
              w_router[l], b_router[l], w_gate_up[l], b_gate_up[l], w_down[l], b_down[l])
        s0_p = jnp.zeros((x_prompt.shape[0], H_A, DK_A, DV_A), jnp.float32)
        y_p, s_p, k_p, v_p = _trunk_layer(y_p, c_prompt, s0_p, None, None, None, l, lb_all[l], *wl)
        y_s, s_s, k_s, v_s = _trunk_layer(y_s, c_sample, state_hgrn[l], cache_k[l], cache_v[l], page_table,
                                          l, lb_all[l], *wl)
        k_p_list.append(k_p)
        v_p_list.append(v_p)
        s_p_list.append(s_p)
        k_s_list.append(k_s)
        v_s_list.append(v_s)
        s_s_list.append(s_s)
    return (y_p, y_s, jnp.stack(k_p_list), jnp.stack(v_p_list), jnp.stack(s_p_list),
            jnp.stack(k_s_list), jnp.stack(v_s_list), jnp.stack(s_s_list))


_drawn_inputs = setup_inputs


def setup_inputs(seed=0):
    import zlib

    import numpy as np

    out = dict(_drawn_inputs(seed))
    spreads = {}
    factors = {'g_post_ffn': 3.897,
     'g_hgrn': 2.857,
     'lam_q1': 3.112,
     'lam_k1': 5.121,
     'lam_q2': 5.221,
     'lam_k2': 8.0,
     'b_router': 3.098,
     'b_gate_up': 8.0,
     'b_down': 8.0}
    for name, (base, spread) in spreads.items():
        noise = np.random.default_rng([zlib.crc32(name.encode()), seed]).standard_normal(out[name].shape)
        drawn = base * np.exp(spread * noise) if base else spread * noise
        out[name] = __import__('jax').numpy.asarray(drawn.astype(out[name].dtype))
    for name, factor in factors.items():
        out[name] = (out[name] * factor).astype(out[name].dtype)
    return out
```

```python
from contextlib import ExitStack

import numpy as np

import concourse.bass as bass
from concourse import mybir

F32 = mybir.dt.float32
BF16 = mybir.dt.bfloat16
I32 = mybir.dt.int32
U32 = mybir.dt.uint32
ALU = mybir.AluOpType
ACT = mybir.ActivationFunctionType
AX = mybir.AxisListType.X

P = 128
D = 1024
KC = D // P
TP = 256
NS = 8
T = TP + NS
NCH = 3
H = 4
DV = 128
W = H * DV
CHUNK = 64
NHC = TP // CHUNK
PAGE = 128
NPG = 2
PAST = NPG * PAGE
E = 32
TOPK = 4
M = 64
MAXB = E + T * TOPK // M
LIMIT = 7.0
ALPHA = 1.702
EPS = 1e-6
LAM_INIT = 0.2
NEG = -1e30
SLOT = 2048
D_IN = 5632

CONST_WIDTHS = [("ident", 128), ("ones", 128), ("tri", 128), ("iota_slot", M), ("iota_e", E),
                ("causal", 128), ("bias", H * 384), ("scan", T), ("sbias", PAST + 1), ("pair", 32),
                ("selp", 128), ("sels", NS), ("maps", 2), ("lamc", 2), ("onehot_e", E)]
CONST = {}
_at = 0
for _n, _w in CONST_WIDTHS:
    CONST[_n] = (_at, _w)
    _at += _w
NCONST = _at


def constants():
    c = np.zeros((P, NCONST), np.float32)

    def put(name, a):
        at, w = CONST[name]
        c[: a.shape[0], at:at + w] = a

    p = np.arange(P)
    put("ident", np.eye(P))
    put("ones", np.ones((P, P)))
    put("tri", (p[:, None] < p[None, :]).astype(np.float32))
    put("iota_slot", np.tile(np.arange(M), (P, 1)))
    put("iota_e", np.tile(np.arange(E), (P, 1)))
    put("causal", ((p[:, None] // CHUNK == p[None, :] // CHUNK) & (p[:, None] <= p[None, :])))
    slopes = 2.0 ** (-8.0 * np.arange(1, H + 1) / H)
    bias = np.zeros((P, H, 384))
    for h in range(H):
        for lo, q0, n in ((0, 0, 128), (128, 128, 256)):
            dist = (q0 + p)[:, None] - np.arange(n)[None, :]
            bias[:, h, lo:lo + n] = np.where(dist >= 0, -slopes[h] * dist, NEG)
    put("bias", bias.reshape(P, -1))
    put("scan", np.tile((np.arange(T) % CHUNK != 0) & (np.arange(T) < TP), (P, 1)))
    r = np.arange(64)
    put("sbias", -slopes[(r // 2) % H][:, None] * (PAST - np.arange(PAST + 1))[None, :])
    put("pair", (r[:, None] // 2 == np.arange(32)[None, :]).astype(np.float32))
    put("selp", np.repeat((p % 32 == 0)[:, None], P, 1).astype(np.float32))
    put("sels", (p[:, None] % 32 == 1 + np.arange(NS)[None, :]).astype(np.float32))
    put("maps", np.stack([p < 64, p >= 64], 1).astype(np.float32))
    put("lamc", np.stack([p % 2 == 0, p % 2 == 1], 1).astype(np.float32))
    put("onehot_e", (p[:, None] % E == np.arange(E)[None, :]).astype(np.float32))
    return c


UNITS = ([("mod", 0, i) for i in range(4)] + [("in", 0), ("in", 1)]
         + [("mod", 1, i) for i in range(4)] + [("in", 2), ("in", 3)]
         + [("mod", 2, i) for i in range(4)] + [("in", u) for u in range(4, 11)]
         + [("pa",), ("pb",), ("wo", 0), ("wo", 1)])
UNIT_AT = {u: n for n, u in enumerate(UNITS)}
NU = len(UNITS)

AUX_ORDER = (["vt", "mt0"] + [f"xt{k}" for k in range(KC)] + ["mt1", "mt2"]
             + ["kt0", "kt1", "as0", "as1"] + [f"kv{c}" for c in range(NHC)]
             + [f"oa{h}" for h in range(H)]
             + ["vas", "kks"] + [f"ou{h}{b}" for h in range(H) for b in range(2)]
             + ["tok0", "tok1", "toks", "qs", "vbs"]
             + [f"sc{h}{m}" for h in range(H) for m in range(2)]
             + [f"pt{h}" for h in range(H)] + [f"ob{h}" for h in range(H)]
             + [f"qb{b}" for b in range(NS)] + ["ss", "pd"]
             + [f"n{x}{i}" for x in "ab" for i in range(3)]
             + ["g1p0", "g1p1", "g1s0", "g1s1"]
             + [f"h2t{k}" for k in range(KC)] + [f"h2r{c}{i}" for c in range(NCH) for i in range(2)]
             + ["rt0", "rt1", "rt2", "pos", "g2p0", "g2p1", "g2s0", "g2s1"])
AUX = {n: i for i, n in enumerate(AUX_ORDER)}
PROJ_ORDER = ([f"aq{j}" for j in range(4)] + [f"af{j}" for j in range(4)] + ["va0", "va1", "vas"]
              + [f"ag{j}" for j in range(4)] + [f"bq{j}" for j in range(4)]
              + [f"bk{j}" for j in range(4)] + ["vb0", "vb1", "vbs"]
              + [f"ga{j}" for j in range(8)] + [f"gb{j}" for j in range(8)])
PROJ = {n: i for i, n in enumerate(PROJ_ORDER)}
NPROJ = len(PROJ_ORDER)


def build(nc, a, o):
    ctx = ExitStack()
    with ctx:
        def sb(name, shape, dt=F32):
            return ctx.enter_context(nc.sbuf_tensor(name, shape, dt))

        sems = {}

        def S(name):
            if name not in sems:
                sems[name] = ctx.enter_context(nc.semaphore(name))
            return sems[name]

        ring = sb("ring", [P, 4 * SLOT])
        late = sb("late", [P, 8 * SLOT])
        cst = sb("cst", [P, NCONST])
        x = sb("x", [P, NCH, D])
        wide = sb("wide", [P, NCH * D])
        hT = sb("hT", [P, KC, T])
        mod = sb("mod", [P, 3, 512])
        gpost = sb("gpost", [P, 512])
        G = sb("G", [P, 2, D])
        va = sb("va", [P, 2, W])
        vas = sb("vas", [NS, W])
        vb = sb("vb", [P, 2, W])
        vbs = sb("vbs", [NS, W])
        gates = sb("gates", [P, 2 * KC * T])
        agT = sb("agT", [P, H, T])
        att = sb("att", [P, 2, 384])
        tok = sb("tok", [P, W])
        biases = sb("biases", [96, 3 * D], BF16)
        sel = sb("sel", [96, M], BF16)
        small = sb("small", [P, 640])
        A1 = sb("A1", [P, KC, 9])
        SH1 = sb("SH1", [P, KC, 9])
        A2 = sb("A2", [P, KC, 9])
        SH2 = sb("SH2", [P, KC, 9])
        gint = sb("gint", [P, NCH * TOPK], I32)
        tab = sb("tab", [1, E + 1], I32)
        used_tab = sb("used_tab", [1, E], I32)
        pgt = sb("pgt", [1, NS * NPG], I32)
        ybuf = nc.dram_tensor("ybuf", (MAXB * M, D), F32, kind="Internal").ap()
        PB = [ctx.enter_context(nc.psum_tensor(f"PB{i}", [P, 512], F32)) for i in range(8)]

        def C(name, rows=P):
            at, w = CONST[name]
            return cst[0:rows, at:at + w]

        ident = C("ident")
        def late_tile(i, n=H * T):
            return late[:, i * H * T:i * H * T + n]

        AQ, FG, LN, GC, KK, KD, ET, OA, OB = (
            late_tile(i).rearrange("p (h t) -> p h t", h=H) for i in range(9))
        base = 9 * H * T
        SA = late[:, base:base + NHC * W].rearrange("p (c h v) -> p c h v", c=NHC, h=H)
        S0 = late[:, base + 2048:base + 4096].rearrange("p (s b v) -> p s b v", s=2, b=NS)
        QT = late[:, base + 4096:base + 4096 + H * T].rearrange("p (h t) -> p h t", h=H)
        at = base + 4096 + H * T
        KT_ = late[:, at:at + H * T].rearrange("p (h t) -> p h t", h=H)
        ET_rows = late_tile(6, 2 * W).rearrange("p (c n) -> p c n", c=2)
        A_rows = late_tile(8, 2 * W).rearrange("p (c h t) -> p c h t", c=2, h=H)

        def pr(h):
            return late[:, 2 * H * T + h * 384:2 * H * T + (h + 1) * 384]

        qs_rows = vas
        hTf = hT[:, :, :].rearrange("p k t -> p (k t)")
        eps = sb("eps", [P, 1])
        VTs = sb("VTs", [P, 72])
        AQf, FGf, LNf, GCf, KKf, KDf, ETf, OAf, OBf = (late_tile(i) for i in range(9))
        xn = wide[:, :].rearrange("p (c d) -> p c d", c=NCH)
        kpg = wide[:, 0:2048].rearrange("p (s g n) -> p s g n", s=2, g=NPG)
        vm = wide[0:NS, 2048:3072].rearrange("p (b v) -> p b v", b=NS)
        prod = wide[:, 2048:3072].rearrange("p (g n) -> p g n", g=NPG)
        vpg = G[:, :, :].rearrange("p s (g n) -> p s g n", g=NPG)
        gaT = gates[:, 0:KC * T].rearrange("p (s t) -> p s t", s=KC)
        gbT = gates[:, KC * T:2 * KC * T].rearrange("p (s t) -> p s t", s=KC)
        bias_f = gates[0:E, 0:3 * D]
        bias_t = gates[0:E, 3 * D:4 * D]
        wr = sb("wr", [P, KC, E])
        br = sb("br", [P, E])
        lamv = sb("lamv", [P, 4, 64])
        vrows = sb("vrows", [P, P])
        VT = sb("VT", [P, P])
        VC, VG1, VG2, VLB, VGA, VGB, NV = 0, 72, 80, 88, 96, 100, 101
        cT = sb("cT", [P, KC, 32])
        at += H * T
        assert at + 612 <= 8 * SLOT
        ssm = late[:, at:at + 612]
        sS = ssm[:, 0:128].rearrange("p (g r) -> p g r", g=NPG)
        sP = ssm[0:64, 128:128 + PAST + 1]
        sC = ssm[0:64, 388:420]
        sD = ssm[:, 420:516]
        self_prod = ssm[:, 516:548].rearrange("p (b h) -> p b h", b=NS)
        self_lhs = ssm[:, 548:612]
        self_lhs4 = self_lhs.rearrange("p (b h m) -> p b h m", b=NS, h=H)
        sPb = att[0:64, 0, 0:P]

        sm = {}
        at = 0
        for n, w in (("ssq", 3), ("rs", 3), ("lb", 12), ("omlb", 4), ("lam", 8), ("egl", 16), ("nm", 16),
                     ("l", 16), ("r", 16), ("snm", 1), ("sl", 1), ("sr", 1), ("top", 24), ("idx", 24),
                     ("idf", 24), ("ge", 12), ("gs", 3), ("gr", 3), ("g", 12), ("grel", 12),
                     ("nb", 32), ("incl", 32), ("cmp", 32), ("y2", 6), ("vaT", 32), ("vbT", 32),
                     ("osa", 32), ("osb", 32), ("gsl", 1), ("xs", 64), ("coef", 1), ("one", 1), ("big", 40)):
            sm[n] = (at, w)
            at += w
        assert at <= 640, at

        def sv(n, lo=0, hi=None, rows=P, r0=0):
            s, w = sm[n]
            return small[r0:rows, s + lo:s + (w if hi is None else hi)]

        mo = {}
        at = 0
        for n, w in (("glu", 512), ("lin", 512), ("sig", 512), ("actm", 512), ("xT", 512), ("actT", 512),
                     ("y", 512), ("Pm", NCH * M)):
            mo[n] = gates[:, at:at + w]
            at += w
        assert at <= 2 * KC * T
        eqt = att[:, :, :].rearrange("p m n -> p (m n)")
        vaf = va[:, :, :].rearrange("p c n -> p (c n)")
        onehot = vaf[:, 0:384].rearrange("p (c k e) -> p c k e", c=NCH, k=TOPK)
        mask = vaf[:, 384:480].rearrange("p (c e) -> p c e", c=NCH)
        lg = vaf[:, 480:576].rearrange("p (c e) -> p c e", c=NCH)

        def ring_unit(n):
            return ring[:, (n % 2) * 2 * SLOT:(n % 2 + 1) * 2 * SLOT]

        def slot(i):
            return ring[:, i * SLOT:(i + 1) * SLOT] if i < 4 else late[:, (i - 4) * SLOT:(i - 3) * SLOT]

        def aux(name):
            return PB[5 + AUX[name] % 3]

        rows_of = [P, P, NS]

        def after_unit(n):
            u = UNITS[n]
            if u[0] == "mod":
                return "mod_used", 4 * u[1] + u[2] + 1
            if u[0] == "in":
                last = ["aq3", "af3", "vas", "ag3", "bq3", "bk3", "vbs", "ga3", "ga7", "gb3", "gb7"][u[1]]
                return "proj_full", PROJ[last] + 1
            return ("merge_full", KC) if u[0] in ("pa", "pb") else ("yo_full", NCH)

        block = ctx.enter_context(nc.Block())

        @block.sync
        def _(sp):
            wmod = a["w_mod"][0].rearrange("(k p) n -> p k n", p=P)
            win = a["w_in"][0].rearrange("(k p) n -> p k n", p=P)
            for n, u in enumerate(UNITS):
                if n >= 2:
                    sem, value = after_unit(n - 2)
                    sp.wait_ge(S(sem), value)
                dst = ring_unit(n)
                if u[0] == "mod":
                    src = wmod[:, 2 * u[2]:2 * u[2] + 2, u[1] * 2048:(u[1] + 1) * 2048]
                    dst = dst.rearrange("p (k n) -> p k n", k=2)
                elif u[0] == "in":
                    src = win[:, :, u[1] * 512:(u[1] + 1) * 512]
                    dst = dst.rearrange("p (k n) -> p k n", k=KC)
                elif u[0] in ("pa", "pb"):
                    src = a["w_proj_a" if u[0] == "pa" else "w_proj_b"][0].rearrange("(h p) n -> p h n", p=P)
                    dst = dst.rearrange("p (h n) -> p h n", h=H)
                else:
                    src = a["w_out"][0, u[1] * 512:(u[1] + 1) * 512, :].rearrange("(k p) n -> p k n", p=P)
                    dst = dst.rearrange("p (k n) -> p k n", k=4)
                sp.dma_start(dst, src).then_inc(S(f"unit{n % 2}_landed"), 16)

            def load_expert(e, u):
                if u < 8:
                    src = a["w_gate_up"][0, bass.ds(e, 1) if not isinstance(e, int) else slice(e, e + 1), u * P:(u + 1) * P, :]
                    src = src.rearrange("e p n -> p (e n)")
                    dst = slot(u)
                else:
                    src = a["w_down"][0, bass.ds(e, 1) if not isinstance(e, int) else slice(e, e + 1), (u - 8) * 2 * P:(u - 7) * 2 * P, :]
                    src = src.rearrange("e (k p) n -> p (e k) n", p=P)
                    dst = slot(u).rearrange("p (k n) -> p k n", k=2)
                sp.dma_start(dst, src).then_inc(S(f"w{u}_landed"), 16)

            sp.wait_ge(S("merge_full"), KC)
            sp.wait_ge(S("st_stored"), 16 * (H + 1))
            for u in range(4, 12):
                load_expert(0, u)
            sp.wait_ge(S("yo_full"), NCH)
            for u in range(4):
                load_expert(0, u)
            sp.wait_ge(S("tab_ready"), 1)
            with sp.Fori(1, E) as e:
                before = sp.value_load(used_tab[0:1, bass.ds(e, 1)], min_val=0, max_val=12 * MAXB)
                for u in range(12):
                    sp.wait_ge(S("w_used"), before + (u + 1))
                    load_expert(e, u)

        @block.gpsimd
        def _(pool):
            pool.dma_start(pgt[0:1, :], a["page_table"].rearrange("(a b) n -> a (b n)", a=1)).then_inc(S("pg_loaded"), 16)
            for j in range(4):
                b = a["b_mod"]
                src = bass.AP(b.tensor, j * 512, [[0, 32], [2048, 3], [1, 512]])
                pool.dma_start(mod[32 * j:32 * j + 32, :, :], src).then_inc(S("bmod_loaded"), 16)
                g = a["g_post_mix"] if j < 2 else a["g_post_ffn"]
                src = bass.AP(g.tensor, (j % 2) * 512, [[0, 32], [1, 512]])
                pool.dma_start(gpost[32 * j:32 * j + 32, :], src).then_inc(S("gpost_loaded"), 16)
            pool.dma_start(bias_f[:, 0:2 * D], a["b_gate_up"][0]).then_inc(S("bias_loaded"), 16)
            pool.dma_start(bias_f[:, 2 * D:3 * D], a["b_down"][0]).then_inc(S("bias_loaded"), 16)
            for i, n in enumerate(("lam_q1", "lam_k1", "lam_q2", "lam_k2")):
                pool.dma_start(lamv[:, i, :], bass.AP(a[n].tensor, 0, [[0, P], [1, 64]])).then_inc(S("lam_loaded"), 16)
            pool.dma_start(wr[:, :, :], a["w_router"][0].rearrange("(k p) e -> p k e", p=P)).then_inc(S("wr_loaded"), 16)
            pool.dma_start(br[:, :], bass.AP(a["b_router"].tensor, 0, [[0, P], [1, E]])).then_inc(S("wr_loaded"), 16)

            st_in = a["state_hgrn"][0].rearrange("b h k v -> h k b v")
            st_out = o[7][0].rearrange("b h k v -> h k b v")
            for h in range(2):
                pool.dma_start(S0[:, h, :, :], st_in[h]).then_inc(S(f"s0_{h}_loaded"), 16)
            pool.wait_ge(S("pg_loaded"), 16)

            def pages(b, dst, cache, sem):
                for g in range(NPG):
                    page = pool.value_load(pgt[0:1, b * NPG + g:b * NPG + g + 1], min_val=0,
                                           max_val=a["cache_k"].shape[1] - 1)
                    src = a[cache][0, bass.ds(page, 1), :, :, :].rearrange("a p h n -> p (a h n)")
                    pool.dma_start(dst[:, b % 2, g, :], src).then_inc(S(f"{sem}{b % 2}_loaded"), 16)

            pool.wait_ge(S("state_ready"), 1)
            pool.dma_start(o[4][0, 0].rearrange("h k v -> k h v"), SA[:, NHC - 1, :, :]).then_inc(S("st_stored"), 16)
            for h in range(H):
                pool.wait_ge(S("s0_ready"), h + 1)
                pool.dma_start(st_out[h], S0[:, h % 2, :, :]).then_inc(S("st_stored"), 16)
                if h + 2 < H:
                    pool.wait_ge(S("st_stored"), 16 * (h + 2))
                    pool.wait_ge(S("osa_used"), h + 1)
                    pool.dma_start(S0[:, h % 2, :, :], st_in[h + 2]).then_inc(S(f"s0_{h % 2}_loaded"), 16)
            pool.wait_ge(S("vm_done"), H)
            for b in range(NS):
                if b >= 2:
                    pool.wait_ge(S("k_used"), b - 1)
                pages(b, kpg, "cache_k", "k")
            for b in range(NS):
                if b >= 2:
                    pool.wait_ge(S("v_used"), b - 1)
                pages(b, vpg, "cache_v", "v")
            pool.wait_ge(S("tab_ready"), 1)
            at, _w = CONST["onehot_e"]
            pool.tensor_copy(sel[:, :], cst[0:96, at:at + 1].to_broadcast([96, M])).then_inc(S("sel_ready"), 1)
            with pool.Fori(1, E) as e:
                first = pool.value_load(tab[0:1, bass.ds(e, 1)], min_val=0, max_val=MAXB)
                pool.wait_ge(S("y_done"), first)
                pool.tensor_copy(sel[:, :], cst[0:96, bass.ds(e + at, 1)].to_broadcast([96, M])).then_inc(S("sel_ready"), 1)
            pool.wait_ge(S("y_all_stored"), 1)
            for c in range(NCH):
                n = rows_of[c]
                for k in range(TOPK):
                    i = c * TOPK + k
                    dst = ring[0:n, i * D:(i + 1) * D] if i < 8 else late[0:n, (i - 8) * D:(i - 7) * D]
                    pool.indirect_dma_start(
                        out=dst, out_offset=None, in_=ybuf,
                        in_offset=bass.IndirectOffsetOnAxis(ap=gint[0:n, i:i + 1].bitcast(U32), axis=0),
                    ).then_inc(S(f"rows{i}_loaded"), 16)

        @block.tensor
        def _(pe):
            def begin(name):
                if AUX[name] >= 3:
                    pe.wait_ge(S("aux_free"), AUX[name] - 2)
                return aux(name)

            def full(mm):
                mm.then_inc(S("aux_full"), 1)

            def unit(*key):
                n = UNIT_AT[key]
                pe.wait_ge(S(f"unit{n % 2}_landed"), 16 * (n // 2 + 1))
                return ring_unit(n)

            def tr(out, in_, n=P):
                return pe.transpose(out, in_, ident[0:n, 0:n])

            pe.wait_ge(S("small_loaded"), 16 * 8)
            full(tr(begin("vt")[:, 0:NV], vrows[0:NV, :], NV))

            def mod_group(g):
                if g == 0:
                    pe.wait_ge(S("cT_ready"), 1)
                if g:
                    pe.wait_ge(S("mod_free"), g)
                for i in range(4):
                    w = unit("mod", g, i)
                    for kk in range(2):
                        k = 2 * i + kk
                        for j in range(4):
                            mm = pe.matmul(PB[4][32 * j:32 * j + 32, :], cT[:, k, :],
                                           w[:, kk * 2048 + j * 512:kk * 2048 + (j + 1) * 512],
                                           start=(k == 0), stop=(k == KC - 1))
                    mm.then_inc(S("mod_used"), 1)

            def mod_cols(name, g):
                pe.wait_ge(S("mod_free"), g + 1)
                bank = begin(name)
                for q in range(4):
                    mm = tr(bank[:, q * P:(q + 1) * P], mod[:, g, q * P:(q + 1) * P])
                full(mm)

            def proj_bank(name):
                i = PROJ[name]
                if i >= 4:
                    pe.wait_ge(S("proj_free"), i - 3)
                return PB[i % 4]

            def in_T(u, names):
                w = unit("in", u)
                for j, name in enumerate(names):
                    bank = proj_bank(name)
                    for k in range(KC):
                        mm = pe.matmul(bank[:, 0:T], w[:, k * 512 + j * P:k * 512 + (j + 1) * P], hT[:, k, :],
                                       start=(k == 0), stop=(k == KC - 1))
                    mm.then_inc(S("proj_full"), 1)

            def in_tok(u, names):
                w = unit("in", u)
                for c in range(2):
                    bank = proj_bank(names[c])
                    for k in range(KC):
                        mm = pe.matmul(bank[:, :], hT[:, k, c * P:(c + 1) * P], w[:, k * 512:(k + 1) * 512],
                                       start=(k == 0), stop=(k == KC - 1))
                    mm.then_inc(S("proj_full"), 1)
                bank = proj_bank(names[2])
                for j in range(4):
                    for k in range(KC):
                        mm = pe.matmul(bank[:, j * NS:(j + 1) * NS], w[:, k * 512 + j * P:k * 512 + (j + 1) * P],
                                       hT[:, k, TP:T], start=(k == 0), stop=(k == KC - 1))
                mm.then_inc(S("proj_full"), 1)
    
            def feature_major(prefix, ready, first):
                for k in range(KC):
                    if k == 0:
                        pe.wait_ge(S(ready), 1)
                    bank = begin(f"{prefix}{k}")
                    for c in range(NCH):
                        n = rows_of[c]
                        mm = tr(bank[:, c * P:c * P + n], first[0:n, c, k * P:(k + 1) * P], n)
                    full(mm)

            mod_group(0)
            mod_cols("mt0", 0)
            feature_major("xt", "xn_ready", xn)
            pe.wait_ge(S("hT_ready"), 1)
            in_T(0, [f"aq{j}" for j in range(4)])
            in_T(1, [f"af{j}" for j in range(4)])
            mod_group(1)
            in_tok(2, ["va0", "va1", "vas"])
            in_T(3, [f"ag{j}" for j in range(4)])
            mod_group(2)
            mod_cols("mt1", 1)
            mod_cols("mt2", 2)
            in_T(4, [f"bq{j}" for j in range(4)])
            in_T(5, [f"bk{j}" for j in range(4)])
            in_tok(6, ["vb0", "vb1", "vbs"])

            pe.wait_ge(S("hg_k2"), 1)
            for c in range(2):
                bank = begin(f"kt{c}")
                for h in range(H):
                    mm = tr(bank[:, h * P:(h + 1) * P], LN[:, h, c * P:(c + 1) * P])
                full(mm)
            pe.wait_ge(S("hg_qk"), 1)
            for c in range(2):
                bank = begin(f"as{c}")
                for h in range(H):
                    mm = pe.matmul(bank[:, h * P:(h + 1) * P], KD[:, h, c * P:(c + 1) * P],
                                   AQ[:, h, c * P:(c + 1) * P], start=True, stop=True)
                full(mm)
            pe.wait_ge(S("k2_rows"), 2)
            for c in range(NHC):
                bank = begin(f"kv{c}")
                r = (c % 2) * CHUNK
                for h in range(H):
                    mm = pe.matmul(bank[:, h * P:(h + 1) * P],
                                   ET_rows[r:r + CHUNK, c // 2, h * P:(h + 1) * P],
                                   va[r:r + CHUNK, c // 2, h * P:(h + 1) * P], start=True, stop=True)
                full(mm)
            in_T(7, [f"ga{j}" for j in range(4)])
            pe.wait_ge(S("state_ready"), 1)
            for h in range(H):
                bank = begin(f"oa{h}")
                for c in range(2):
                    mm = pe.matmul(bank[:, c * P:(c + 1) * P], va[:, c, h * P:(h + 1) * P],
                                   A_rows[:, c, h, :], start=True, stop=False)
                    for i in range(2):
                        g = 2 * c + i
                        if g:
                            mm = pe.matmul(bank[:, g * CHUNK:(g + 1) * CHUNK], SA[:, g - 1, h, :],
                                           AQ[:, h, g * CHUNK:(g + 1) * CHUNK], start=False, stop=(i == 1))
                full(mm)
            in_T(8, [f"ga{j}" for j in range(4, 8)])
            bank = begin("vas")
            for h in range(H):
                mm = tr(bank[0:NS, h * P:(h + 1) * P], sv("vaT", h * NS, (h + 1) * NS))
            full(mm)
            bank = begin("kks")
            for h in range(H):
                mm = tr(bank[0:NS, h * P:(h + 1) * P], KK[:, h, TP:T])
            full(mm)
            for h in range(H):
                pe.wait_ge(S("vm_ready"), h + 1)
                for b in range(2):
                    bank = begin(f"ou{h}{b}")
                    full(pe.matmul(bank[:, :], tok[0:NS, h * P:(h + 1) * P], vm[:, 4 * b:4 * b + 4, :],
                                   start=True, stop=True))
                pe.wait_ge(S("s0_ready"), h + 1)
                for b in range(NS):
                    mm = pe.matmul(PB[4][:, h * NS + b:h * NS + b + 1], S0[:, h % 2, b, :],
                                   AQ[:, h, TP + b:TP + b + 1], start=True, stop=True)
                mm.then_inc(S("osa_used"), 1)
            in_T(9, [f"gb{j}" for j in range(4)])
            for c in range(2):
                bank = begin(f"tok{c}")
                for h in range(H):
                    mm = tr(bank[:, h * P:(h + 1) * P], KT_[:, h, c * P:(c + 1) * P])
                full(mm)
            bank = begin("toks")
            for h in range(H):
                mm = tr(bank[0:NS, h * P:(h + 1) * P], KT_[:, h, TP:T])
            full(mm)
            bank = begin("qs")
            for h in range(H):
                mm = tr(bank[0:NS, h * P:(h + 1) * P], QT[:, h, TP:T])
            full(mm)
            bank = begin("vbs")
            for h in range(H):
                mm = tr(bank[0:NS, h * P:(h + 1) * P], sv("vbT", h * NS, (h + 1) * NS))
            full(mm)
            for h in range(H):
                for m in range(2):
                    bank = begin(f"sc{h}{m}")
                    q, kk = QT[64 * m:64 * m + 64, h, :], KT_[64 * m:64 * m + 64, h, :]
                    pe.matmul(bank[:, 0:P], q[:, 0:P], kk[:, 0:P], start=True, stop=True)
                    full(pe.matmul(bank[:, P:3 * P], q[:, P:2 * P], kk[:, 0:2 * P], start=True, stop=True))
            in_T(10, [f"gb{j}" for j in range(4, 8)])
            for h in range(H):
                pe.wait_ge(S("pd_ready"), h + 1)
                bank = begin(f"pt{h}")
                for i in range(3):
                    mm = tr(bank[:, i * P:(i + 1) * P], pr(h)[:, i * P:(i + 1) * P])
                full(mm)
            for h in range(H):
                bank = begin(f"ob{h}")
                pe.wait_ge(S("aux_free"), AUX[f"pt{h}"] + 1)
                v = vb[:, :, h * P:(h + 1) * P]
                pe.matmul(bank[:, 0:P], v[:, 0, :], pr(h)[:, 0:P], start=True, stop=True)
                pe.matmul(bank[:, P:2 * P], v[:, 0, :], pr(h)[:, P:2 * P], start=True, stop=False)
                full(pe.matmul(bank[:, P:2 * P], v[:, 1, :], pr(h)[:, 2 * P:3 * P], start=False, stop=True))
            pe.wait_ge(S("aux_free"), AUX["qs"] + 1)
            for b in range(NS):
                full(pe.matmul(begin(f"qb{b}")[:, :], ident[0:NS, b:b + 1].to_broadcast([NS, P]), qs_rows[0:NS, :],
                               start=True, stop=True))
            bank = begin("ss")
            pe.wait_ge(S("self_ready"), 1)
            for g in range(NPG):
                pe.wait_ge(S("k_used"), NS)
                tr(bank[0:64, g * P:(g + 1) * P], sS[:, g, :])
            full(pe.matmul(bank[0:64, PAST:PAST + 1], self_lhs, C("ones")[:, 0:1], start=True, stop=True))
            bank = begin("pd")
            pe.wait_ge(S("pair_ready"), 1)
            for g in range(NPG):
                pe.matmul(bank[:, g * 32:(g + 1) * 32], sP[:, g * P:(g + 1) * P], sC, start=True, stop=True)
            full(pe.matmul(bank[:, 64:96], sPb, sC, start=True, stop=True))
            pe.wait_ge(S("aux_free"), AUX["pd"] + 1)
            for b in range(NS):
                pe.wait_ge(S(f"v{b % 2}_loaded"), 32 * (b // 2 + 1))
                for h in range(H):
                    for g in range(NPG):
                        mm = pe.matmul(PB[4][:, 64 + h * NS + b:65 + h * NS + b], vpg[:, b % 2, g, h * P:(h + 1) * P],
                                       sD[:, g * 32 + b * H + h:g * 32 + b * H + h + 1],
                                       start=(g == 0), stop=(g == NPG - 1))
                mm.then_inc(S("v_used"), 1)
            for xname, sq, ready in (("a", ETf, "sqa_ready"), ("b", KDf, "sqb_ready")):
                pe.wait_ge(S(ready), 1)
                for i in range(3):
                    full(pe.matmul(begin(f"n{xname}{i}")[:, 0:352], C("ones"), sq[:, i * 352:(i + 1) * 352],
                                   start=True, stop=True))
            pe.wait_ge(S("proj_free"), NPROJ)
            pe.wait_ge(S("oF_ready"), 2)
            wpa = unit("pa")
            wpb = unit("pb")
            for s in range(KC):
                if s >= 2:
                    pe.wait_ge(S("merge_free"), s - 1)
                for i, (w, src) in enumerate(((wpa, OA), (wpb, OB))):
                    for h in range(H):
                        mm = pe.matmul(PB[2 * (s % 2) + i][:, 0:T], w[:, h * D + s * P:h * D + (s + 1) * P],
                                       src[:, h, :], start=(h == 0), stop=(h == H - 1))
                mm.then_inc(S("merge_full"), 1)
            def spread(kind, tile, j0):
                for who, sl, n in (("p", C("selp"), P), ("s", C("sels"), NS)):
                    for i in range(2):
                        j = j0 + i
                        mm = pe.matmul(begin(f"{kind}{who}{i}")[0:n, :], sl[32 * j:32 * j + 32, :],
                                       tile[32 * j:32 * j + 32, :], start=True, stop=True, tile_position=(32 * j, 0))
                        full(mm)
            pe.wait_ge(S("grow_ready"), 2)
            spread("g1", mod[:, 1, :], 0)
            pe.wait_ge(S("merge_free"), KC)
            w0 = unit("wo", 0)
            w1 = unit("wo", 1)
            for c in range(NCH):
                n = rows_of[c]
                if c == 2:
                    pe.wait_ge(S("yo_free"), 1)
                for i in range(2):
                    for s in range(KC):
                        w = (w0 if s < 4 else w1)
                        mm = pe.matmul(PB[2 * (c % 2) + i][0:n, :], gaT[:, s, c * P:c * P + n],
                                       w[:, (s % 4) * D + i * 512:(s % 4) * D + (i + 1) * 512],
                                       start=(s == 0), stop=(s == KC - 1))
                mm.then_inc(S("yo_full"), 1)
            feature_major("h2t", "xn2_ready", xn)
            pe.wait_ge(S("hT_ready"), 2)
            for c in range(NCH):
                n = rows_of[c]
                for i in range(2):
                    bank = begin(f"h2r{c}{i}")
                    for k in range(4):
                        mm = tr(bank[0:n, k * P:(k + 1) * P], hT[:, 4 * i + k, c * P:c * P + n])
                    full(mm)
            for c in range(NCH):
                n = rows_of[c]
                bank = begin(f"rt{c}")
                if c == 0:
                    pe.wait_ge(S("wr_loaded"), 32)
                for k in range(KC):
                    mm = pe.matmul(bank[0:n, 0:E], hT[:, k, c * P:c * P + n], wr[:, k, :],
                                   start=(k == 0), stop=(k == KC - 1))
                full(mm)
            pe.wait_ge(S("mask_ready"), 1)
            bank = begin("pos")
            for c in range(NCH + 1):
                for b in range(min(c, NCH - 1) + 1):
                    mm = pe.matmul(bank[:, c * E:(c + 1) * E], C("tri") if b == c else C("ones"), mask[:, b, :],
                                   start=(b == 0), stop=(b == min(c, NCH - 1)))
            full(mm)
            spread("g2", mod[:, 2, :], 2)

            def gather():
                for k in range(KC):
                    for c in range(NCH):
                        mm = pe.matmul(PB[3][:, k * M:(k + 1) * M], xn[:, c, k * P:(k + 1) * P],
                                       mo["Pm"][:, c * M:(c + 1) * M], start=(c == 0), stop=(c == NCH - 1))
                mm.then_inc(S("gathered"), 1)

            pe.wait_ge(S("P_ready"), 1)
            gather()
            pe.wait_ge(S("tab_ready"), 1)
            with pe.Fori(0, E) as e:
                first = pe.value_load(tab[0:1, bass.ds(e, 1)], min_val=0, max_val=MAXB)
                last = pe.value_load(tab[0:1, bass.ds(e + 1, 1)], min_val=1, max_val=MAXB)
                with pe.Fori(first, last) as b:
                    pe.wait_ge(S("xT_ready"), b + 1)
                    for k in range(KC):
                        pe.wait_ge(S(f"w{k}_landed"), (e + 1) * 16)
                        for i in range(2):
                            for half in range(2):
                                mm = pe.matmul(PB[i][64 * half:64 * half + 64, :], mo["xT"][:, k * M:(k + 1) * M],
                                               slot(k)[:, i * D + half * 512:i * D + (half + 1) * 512],
                                               start=(k == 0), stop=False)
                        mm.then_inc(S("w_used"), 1)
                    pe.wait_ge(S("sel_ready"), e + 1)
                    for i in range(2):
                        for half in range(2):
                            mm = pe.matmul(PB[i][64 * half:64 * half + 64, :], sel[:, :],
                                           biases[:, i * D + half * 512:i * D + (half + 1) * 512],
                                           start=False, stop=True)
                    mm.then_inc(S("gu_done"), 1)
                    pe.wait_ge(S("P_ready"), b + 2)
                    gather()
                    pe.wait_ge(S("act_ready"), b + 1)
                    for q in range(4):
                        mm = tr(PB[4][:, q * P:(q + 1) * P], mo["actm"][:, q * P:(q + 1) * P])
                    mm.then_inc(S("actT_done"), 1)
                    pe.wait_ge(S("actT_ready"), b + 1)
                    for k in range(KC):
                        if k % 2 == 0:
                            pe.wait_ge(S(f"w{8 + k // 2}_landed"), (e + 1) * 16)
                        for half in range(2):
                            mm = pe.matmul(PB[2][64 * half:64 * half + 64, :],
                                           mo["actT"][:, (k % 4) * P + (k // 4) * M:(k % 4) * P + (k // 4) * M + M],
                                           slot(8 + k // 2)[:, (k % 2) * D + half * 512:(k % 2) * D + (half + 1) * 512],
                                           start=(k == 0), stop=False)
                        if k % 2:
                            mm.then_inc(S("w_used"), 1)
                    for half in range(2):
                        mm = pe.matmul(PB[2][64 * half:64 * half + 64, :], sel[:, :],
                                       biases[:, 2 * D + half * 512:2 * D + (half + 1) * 512], start=False, stop=True)
                    mm.then_inc(S("y_done"), 1)

        @block.scalar
        def _(act):
            chain = {}

            def do(ins, sem="act_link"):
                chain[sem] = chain.get(sem, 0) + 1
                ins.then_inc(S(sem), 1)
                act.wait_ge(S(sem), chain[sem])

            for dst, src in ((vrows[VC:VC + 8, :], a["c_prompt"].rearrange("a (k p) -> (a k) p", p=P)),
                             (vrows[VC + 8:VC + 72, :], a["c_sample"].rearrange("a (k p) -> (a k) p", p=P)),
                             (vrows[VG1:VG1 + 8, :], a["g_pre_mix"].rearrange("a (k p) -> (a k) p", p=P)),
                             (vrows[VG2:VG2 + 8, :], a["g_pre_ffn"].rearrange("a (k p) -> (a k) p", p=P)),
                             (vrows[VLB:VLB + 8, :], a["hgrn_lb"].rearrange("a (k p) -> (a k) p", p=P)),
                             (vrows[VGA:VGA + 4, :], a["g_hgrn"][0]),
                             (vrows[VGB:VGB + 1, :], a["g_subln"]),
                             (cst[:, :], a["consts"])):
                act.dma_start(dst, src).then_inc(S("small_loaded"), 16)
            act.dma_start(x[:, 0:2, :], a["x_prompt"][0].rearrange("(c p) d -> p c d", p=P)).then_inc(S("x_loaded"), 16)
            act.dma_start(x[0:NS, 2, :], a["x_sample"][:, 0, :]).then_inc(S("x_loaded"), 16)
            act.wait_ge(S("tok_zero"), 1)
            reps = (MAXB - E) * M // P * 2
            act.dma_start(ybuf[E * M:, :].rearrange("(p r) (h n) -> p (r h) n", p=P, n=W),
                          tok[:, :].unsqueeze(1).to_broadcast([P, reps, W])).then_inc(S("y_stored"), 16)
            act.wait_ge(S("x_loaded"), 32)
            act.wait_ge(S("ssq_zero"), 1)
            for c in range(NCH):
                n = rows_of[c]
                do(act.activation(hTf[0:n, 0:D], x[0:n, c, :], ACT.Square,
                                  accum_out=sv("ssq", c, c + 1, n)), "ssq_ready")
            do(act.activation(sv("rs"), sv("ssq"), ACT.Sqrt, scale=1.0 / D, bias=eps[:, :]), "rms_ready")
            act.wait_ge(S("vt_ready"), 1)
            do(act.activation(VTs[:, 0:72], VT[:, 0:72], ACT.Sigmoid), "csig_ready")
            act.wait_ge(S("lbd_ready"), 1)
            do(act.activation(sv("lb", 4, 12), sv("lb", 4, 12), ACT.Exp), "lbe_ready")

            def bank(name):
                i = PROJ[name]
                act.wait_ge(S("proj_full"), i + 1)
                return PB[i % 4]

            for j in range(4):
                do(act.activation(AQ[:, j, :], bank(f"aq{j}")[:, 0:T], ACT.Copy), "proj_free")
            for j in range(4):
                do(act.activation(FG[:, j, :], bank(f"af{j}")[:, 0:T], ACT.Sigmoid), "proj_free")
            do(act.activation(va[:, 0, :], bank("va0")[:, :], ACT.Copy), "proj_free")
            do(act.activation(va[:, 1, :], bank("va1")[:, :], ACT.Copy), "proj_free")
            do(act.activation(sv("vaT"), bank("vas")[:, 0:32], ACT.Copy), "proj_free")
            for j in range(4):
                do(act.activation(OB[:, j, :], bank(f"ag{j}")[:, 0:T], ACT.Sigmoid))
                do(act.activation(agT[:, j, :], bank(f"ag{j}")[:, 0:T], ACT.Copy), "proj_free")
            for j in range(4):
                do(act.activation(QT[:, j, :], bank(f"bq{j}")[:, 0:T], ACT.Copy, scale=0.125), "proj_free")
            act.wait_ge(S("f_ready"), 1)
            do(act.activation(LNf, FGf, ACT.Ln), "ln_ready")
            act.wait_ge(S("gc_ready"), 1)
            do(act.activation(ETf, GCf, ACT.Exp))
            do(act.activation(KDf, GCf, ACT.Exp, scale=-1.0), "eg_ready")
            act.wait_ge(S("gd_ready"), 1)
            do(act.activation(LN[:, :, 0:TP], LN[:, :, 0:TP], ACT.Exp))
            do(act.activation(sv("egl").rearrange("p (h c) -> p h c", h=H),
                              GC[:, :, CHUNK - 1:TP:CHUNK], ACT.Exp), "egl_ready")
            for j in range(4):
                do(act.activation(KT_[:, j, :], bank(f"bk{j}")[:, 0:T], ACT.Copy), "proj_free")
            do(act.activation(vb[:, 0, :], bank("vb0")[:, :], ACT.Copy), "proj_free")
            do(act.activation(vb[:, 1, :], bank("vb1")[:, :], ACT.Copy), "proj_free")
            do(act.activation(sv("vbT"), bank("vbs")[:, 0:32], ACT.Copy), "proj_free")
            act.dma_start(o[3][0, 0].rearrange("(c p) h n -> p c (h n)", p=P), vb[:, :, :]).then_inc(S("out_stored"), 16)
            act.wait_ge(S("bias_split"), 1)
            for j in range(8):
                do(act.activation(gaT[:, j, :], bank(f"ga{j}")[:, 0:T], ACT.Sigmoid), "proj_free")
            for j in range(4):
                do(act.activation(gbT[:, j, :], bank(f"gb{j}")[:, 0:T], ACT.Sigmoid), "proj_free")
            kout = o[2][0, 0].rearrange("(c p) h n -> c p (h n)", p=P)
            for c in range(2):
                act.wait_ge(S("tok_ready"), c + 1)
                act.dma_start(kout[c], tok[:, :]).then_inc(S("tok_stored"), 16)
            act.wait_ge(S("tok_ready"), 3)
            act.dma_start(o[5][0, :, 0].rearrange("b h n -> b (h n)"), tok[0:NS, :]).then_inc(S("tok_stored"), 16)
            act.wait_ge(S("vbs_ready"), 1)
            act.dma_start(o[6][0, :, 0].rearrange("b h n -> b (h n)"), vbs[:, :]).then_inc(S("out_stored"), 16)
            act.wait_ge(S("lam_dots"), 1)
            do(act.activation(sv("lam", 2, 4), sv("lam", 0, 2), ACT.Exp), "lam_exp")
            for h in range(H):
                for m in range(2):
                    i = 2 * h + m
                    act.wait_ge(S("s_ready"), i + 1)
                    for q, (lo, hi) in enumerate(((0, P), (P, 3 * P))):
                        c = 2 * i + q
                        do(act.activation(att[:, m, lo:hi], att[:, m, lo:hi], ACT.Exp, bias=sv("nm", c, c + 1),
                                          accum_out=sv("l", c, c + 1)), "p_ready")
            for j in range(4, 8):
                do(act.activation(gbT[:, j, :], bank(f"gb{j}")[:, 0:T], ACT.Sigmoid), "proj_free")
            act.wait_ge(S("ss_ready"), 1)
            do(act.activation(sP, sP, ACT.Exp, bias=sv("snm", rows=64), accum_out=sv("sl", rows=64)), "sp_ready")
            act.wait_ge(S("oab_ready"), 1)
            do(act.activation(ETf, OAf, ACT.Square), "sqa_ready")
            act.wait_ge(S("oab_ready"), 2)
            do(act.activation(KDf, OBf, ACT.Square), "sqb_ready")
            for i in range(2):
                act.wait_ge(S("ms_ready"), i + 1)
                do(act.activation(GCf, GCf, ACT.Sqrt, bias=eps[:, :]), "hrms_ready")
            for c in range(NCH):
                n = rows_of[c]
                act.wait_ge(S("yo_full"), c + 1)
                for i in range(2):
                    do(act.activation(eqt[0:n, 0:512], PB[2 * (c % 2) + i][0:n, :], ACT.Square,
                                      accum_out=sv("y2", 2 * c + i, 2 * c + i + 1, n)), "y2_ready")
                act.wait_ge(S("y2_summed"), c + 1)
                do(act.activation(sv("rs", c, c + 1, n), sv("rs", c, c + 1, n), ACT.Sqrt, scale=1.0 / D,
                                  bias=eps[0:n, :]), "yrms_ready")
            for c in range(NCH):
                n = rows_of[c]
                act.wait_ge(S("x1_ready"), c + 1)
                do(act.activation(hTf[0:n, 0:D], x[0:n, c, :], ACT.Square,
                                  accum_out=sv("ssq", c, c + 1, n)), "ssq_ready")
            do(act.activation(sv("rs"), sv("ssq"), ACT.Sqrt, scale=1.0 / D, bias=eps[:, :]), "rms_ready")
            for c in range(NCH):
                n = rows_of[c]
                act.wait_ge(S("top_ready"), c + 1)
                do(act.activation(sv("ge", 4 * c, 4 * c + 4, n), sv("top", 8 * c, 8 * c + 4, n), ACT.Exp,
                                  bias=sv("gr", c, c + 1, n), accum_out=sv("gs", c, c + 1, n)), "ge_ready")
            act.wait_ge(S("gathered"), 1)
            act.activation(mo["xT"], PB[3][:, :], ACT.Copy).then_inc(S("xT_ready"), 1)
            act.wait_ge(S("tab_ready"), 1)
            nblocks = act.value_load(tab[0:1, E:E + 1], min_val=1, max_val=MAXB)
            with act.Fori(0, nblocks) as b:
                act.wait_ge(S("glu_ready"), b + 1)
                act.activation(mo["sig"], mo["glu"], ACT.Sigmoid, scale=ALPHA).then_inc(S("sig_ready"), 1)
                act.wait_ge(S("gathered"), b + 2)
                act.activation(mo["xT"], PB[3][:, :], ACT.Copy).then_inc(S("xT_ready"), 1)
                act.wait_ge(S("actT_done"), b + 1)
                act.activation(mo["actT"], PB[4][:, :], ACT.Copy).then_inc(S("actT_ready"), 1)
                act.wait_ge(S("y_done"), b + 1)
                act.wait_ge(S("y_stored"), b * 32 + 16)
                act.activation(mo["y"], PB[2][:, :], ACT.Copy).then_inc(S("y_free"), 1)
                act.wait_ge(S("y_free"), b + 1)
                for half in range(2):
                    act.dma_start(ybuf[bass.ds(b * M, M), half * 512:(half + 1) * 512],
                                  mo["y"][64 * half:64 * half + 64, :]).then_inc(S("y_stored"), 16)
            act.wait_ge(S("y_stored"), nblocks * 32 + 16)
            act.nop().then_inc(S("y_all_stored"), 1)
            for c in range(NCH):
                n = rows_of[c]
                act.wait_ge(S("m_ready"), c + 1)
                do(act.activation(hTf[0:n, 0:D], xn[0:n, c, :], ACT.Square, accum_out=sv("ssq", c, c + 1, n)),
                   "ssq_ready")
                do(act.activation(sv("rs", c, c + 1, n), sv("ssq", c, c + 1, n), ACT.Sqrt, scale=1.0 / D,
                                  bias=eps[0:n, :]), "rms_ready")
            for c in range(NCH):
                act.wait_ge(S("final_ready"), c + 1)
                if c < 2:
                    act.dma_start(o[0][0, c * P:(c + 1) * P, :], xn[:, c, :]).then_inc(S("out_stored"), 16)
                else:
                    act.dma_start(o[1][:, 0, :], xn[0:NS, c, :]).then_inc(S("out_stored"), 16)
            act.wait_ge(S("out_stored"), 16 * 5)
            act.wait_ge(S("tok_stored"), 16 * 3)
            act.wait_ge(S("st_stored"), 16 * (H + 1))

        @block.vector
        def _(dve):
            chain = {}

            def do(ins, sem="dve_link"):
                chain[sem] = chain.get(sem, 0) + 1
                ins.then_inc(S(sem), 1)
                dve.wait_ge(S(sem), chain[sem])

            def bank(name):
                dve.wait_ge(S("aux_full"), AUX[name] + 1)
                return aux(name)

            def ts(out, in_, s1, s2, op0, op1=None, sem="dve_link"):
                do(dve.tensor_scalar(out, in_, s1, s2, op0, op1) if op1 is not None
                   else dve.tensor_scalar(out, in_, s1, None, op0), sem)

            def tt(out, x0, x1, op, sem="dve_link"):
                do(dve.tensor_tensor(out, x0, x1, op), sem)

            def stt(out, x0, s, x1, op0, op1, sem="dve_link"):
                do(dve.scalar_tensor_tensor(out, x0, s, x1, op0, op1), sem)

            def copy(out, in_, sem="dve_link"):
                do(dve.tensor_copy(out, in_), sem)

            do(dve.memset(small[:, :], 0.0))
            do(dve.memset(tok[:, :], 0.0), "tok_zero")
            do(dve.memset(eps[:, :], EPS), "ssq_zero")
            do(dve.memset(cT[:, :, :], 0.0))
            do(dve.memset(sv("g"), -1.0))
            copy(VT[:, 0:NV], bank("vt")[:, 0:NV])
            dve.nop().then_inc(S("aux_free"), 1)
            dve.nop().then_inc(S("vt_ready"), 1)
            l0, l1 = VT[:, VLB:VLB + 4], VT[:, VLB + 4:VLB + 8]
            tt(sv("lb", 0, 4), l0, l1, ALU.max)
            tt(sv("lb", 4, 8), l0, sv("lb", 0, 4), ALU.subtract)
            tt(sv("lb", 8, 12), l1, sv("lb", 0, 4), ALU.subtract)
            dve.nop().then_inc(S("lbd_ready"), 1)
            dve.wait_ge(S("csig_ready"), 1)
            do(dve.tensor_tensor(cT[:, :, 0:9], VT[:, 0:72].rearrange("p (r k) -> p k r", r=9),
                                 VTs[:, 0:72].rearrange("p (r k) -> p k r", r=9), ALU.mult), "cT_ready")
            dve.wait_ge(S("rms_ready"), 1)
            do(dve.reciprocal(sv("rs"), sv("rs")))
            for c in range(NCH):
                n = rows_of[c]
                ts(xn[0:n, c, :], x[0:n, c, :], sv("rs", c, c + 1, n), None, ALU.mult)
            dve.nop().then_inc(S("xn_ready"), 1)
            dve.wait_ge(S("bias_loaded"), 32)
            for i in range(3):
                cols = slice(i * D, (i + 1) * D)
                for part in range(3):
                    copy(biases[32 * part:32 * part + 32, cols], bias_f[:, cols])
                    if part < 2:
                        copy(bias_t, biases[32 * part:32 * part + 32, cols])
                        tt(bias_f[:, cols], bias_f[:, cols], bias_t, ALU.subtract)
            dve.nop().then_inc(S("bias_split"), 1)

            def mod_rows(g):
                dve.wait_ge(S("mod_used"), 4 * g + 4)
                if g == 0:
                    dve.wait_ge(S("bmod_loaded"), 64)
                do(dve.tensor_tensor(mod[:, g, :], PB[4][:, :], mod[:, g, :], ALU.add), "mod_free")

            def scale_cols(A, b4, kind, gains):
                src = b4.rearrange("p (q j r) -> p j q r", q=4, j=4)[:, 2 * kind:2 * kind + 2, :, 0:9]
                for j in range(2):
                    g = VT[:, gains + 4 * j:gains + 4 * j + 4].unsqueeze(2).to_broadcast([P, 4, 9])
                    stt(A[:, 4 * j:4 * j + 4, :], src[:, j], 1.0, g, ALU.add, ALU.mult)

            def shift_cols(SH, b4, kind):
                src = b4.rearrange("p (q j r) -> p j q r", q=4, j=4)[:, 2 * kind:2 * kind + 2, :, 0:9]
                for j in range(2):
                    copy(SH[:, 4 * j:4 * j + 4, :], src[:, j])

            def free():
                dve.nop().then_inc(S("aux_free"), 1)

            def modulate(prefix, A, SH):
                for k in range(KC):
                    b = bank(f"{prefix}{k}")
                    ts(hT[:, k, 0:TP], b[:, 0:TP], A[:, k, 0:1], SH[:, k, 0:1], ALU.mult, ALU.add)
                    tt(hT[:, k, TP:T], b[:, TP:T], A[:, k, 1:9], ALU.mult)
                    free()
                tt(hT[:, :, TP:T], hT[:, :, TP:T], SH[:, :, 1:9], ALU.add)
                dve.nop().then_inc(S("hT_ready"), 1)

            mod_rows(0)
            b = bank("mt0")
            shift_cols(SH1, b, 0)
            scale_cols(A1, b, 1, VG1)
            free()
            modulate("xt", A1, SH1)
            dve.wait_ge(S("lbe_ready"), 1)
            tt(sv("lb", 0, 4), sv("lb", 4, 8), sv("lb", 8, 12), ALU.add)
            do(dve.reciprocal(sv("lb", 0, 4), sv("lb", 0, 4)))
            tt(sv("lb", 0, 4), sv("lb", 4, 8), sv("lb", 0, 4), ALU.mult)
            ts(sv("omlb"), sv("lb", 0, 4), -1.0, 1.0, ALU.mult, ALU.add)
            dve.wait_ge(S("lam_loaded"), 64)
            for i in range(2):
                tt(lamv[:, 2 * i, :], lamv[:, 2 * i, :], lamv[:, 2 * i + 1, :], ALU.mult)
                do(dve.tensor_reduce(sv("lam", i, i + 1), lamv[:, 2 * i, :], AX, ALU.add))
            dve.nop().then_inc(S("lam_dots"), 1)
            dve.wait_ge(S("proj_free"), PROJ["af3"] + 1)
            for h in range(H):
                ts(FG[:, h, :], FG[:, h, :], sv("omlb", h, h + 1), sv("lb", h, h + 1), ALU.mult, ALU.add)
            dve.nop().then_inc(S("f_ready"), 1)
            ts(KKf, FGf, -1.0, 1.0, ALU.mult, ALU.add)
            mod_rows(1)
            dve.wait_ge(S("proj_free"), PROJ["ag3"] + 1)
            tt(agT[:, :, :], agT[:, :, :], OB[:, :, :], ALU.mult)
            do(dve.memset(A_rows, 0.0))
            mod_rows(2)
            shift_cols(SH2, bank("mt1"), 1)
            free()
            scale_cols(A2, bank("mt2"), 0, VG2)
            free()
            dve.wait_ge(S("gpost_loaded"), 64)
            tt(mod[0:64, 1, :], mod[0:64, 1, :], gpost[0:64, :], ALU.mult, "grow_ready")
            tt(mod[64:128, 2, :], mod[64:128, 2, :], gpost[64:128, :], ALU.mult, "grow_ready")
            dve.wait_ge(S("ln_ready"), 1)
            for h in range(H):
                do(dve.tensor_tensor_scan(GC[:, h, :], C("scan"), LN[:, h, :], 0.0, ALU.mult, ALU.add))
            dve.nop().then_inc(S("gc_ready"), 1)
            for h in range(H):
                last = GC[:, h, CHUNK - 1:TP:CHUNK].unsqueeze(2).to_broadcast([P, NHC, CHUNK])
                tt(LN[:, h, 0:TP].rearrange("p (c t) -> p c t", c=NHC), last,
                   GC[:, h, 0:TP].rearrange("p (c t) -> p c t", c=NHC), ALU.subtract)
            dve.nop().then_inc(S("gd_ready"), 1)
            dve.wait_ge(S("eg_ready"), 1)
            tt(AQ[:, :, 0:TP], AQ[:, :, 0:TP], ET[:, :, 0:TP], ALU.mult)
            tt(KDf, KDf, KKf, ALU.mult)
            dve.nop().then_inc(S("hg_qk"), 1)
            dve.wait_ge(S("egl_ready"), 1)
            tt(LN[:, :, 0:TP], LN[:, :, 0:TP], KK[:, :, 0:TP], ALU.mult)
            dve.nop().then_inc(S("hg_k2"), 1)
            for c in range(2):
                copy(ET_rows[:, c, :], bank(f"kt{c}")[:, :], "k2_rows")
                free()
            for c in range(2):
                b = bank(f"as{c}")
                for h in range(H):
                    do(dve.copy_predicated(A_rows[:, c, h, :], C("causal").bitcast(U32), b[:, h * P:(h + 1) * P]))
                free()
            for c in range(NHC):
                b = bank(f"kv{c}")
                for h in range(H):
                    kv = b[:, h * P:(h + 1) * P]
                    if c == 0:
                        copy(SA[:, 0, h, :], kv)
                    else:
                        i = h * NHC + c
                        stt(SA[:, c, h, :], SA[:, c - 1, h, :], sv("egl", i, i + 1), kv, ALU.mult, ALU.add)
                free()
            dve.nop().then_inc(S("state_ready"), 1)
            for h in range(H):
                copy(OA[:, h, 0:TP], bank(f"oa{h}")[:, 0:TP])
                free()
            copy(vas[:, :], bank("vas")[0:NS, :])
            free()
            dve.wait_ge(S("y_stored"), 16)
            copy(tok[0:NS, :], bank("kks")[0:NS, :])
            free()
            for h in range(H):
                tt(vm, vas[:, h * P:(h + 1) * P].unsqueeze(1).to_broadcast([NS, NS, P]),
                   ident[0:NS, 0:NS].unsqueeze(2).to_broadcast([NS, NS, P]), ALU.mult, "vm_ready")
                dve.wait_ge(S(f"s0_{h % 2}_loaded"), 16 * (h // 2 + 1))
                for b2 in range(2):
                    b = bank(f"ou{h}{b2}")
                    for i in range(4):
                        s = 4 * b2 + i
                        stt(S0[:, h % 2, s, :], S0[:, h % 2, s, :], FG[:, h, TP + s:TP + s + 1],
                            b[:, i * P:(i + 1) * P], ALU.mult, ALU.add)
                    free()
                dve.nop().then_inc(S("s0_ready"), 1)
                dve.nop().then_inc(S("vm_done"), 1)
            dve.wait_ge(S("osa_used"), H)
            copy(OA[:, :, TP:T], PB[4][:, 0:H * NS].rearrange("p (h b) -> p h b", h=H))
            dve.nop().then_inc(S("oab_ready"), 1)
            for c in range(2):
                if c:
                    dve.wait_ge(S("tok_stored"), 16 * c)
                copy(tok[:, :], bank(f"tok{c}")[:, :])
                free()
                dve.nop().then_inc(S("tok_ready"), 1)
            dve.wait_ge(S("tok_stored"), 32)
            copy(tok[0:NS, :], bank("toks")[0:NS, :])
            free()
            dve.nop().then_inc(S("tok_ready"), 1)
            copy(qs_rows[0:NS, :], bank("qs")[0:NS, :])
            free()
            copy(vbs[:, :], bank("vbs")[0:NS, :])
            free()
            dve.nop().then_inc(S("vbs_ready"), 1)
            dve.wait_ge(S("lam_exp"), 1)
            tt(sv("lam", 4, 5), sv("lam", 3, 4), sv("lam", 2, 3), ALU.subtract)
            ts(sv("lam", 4, 5), sv("lam", 4, 5), -LAM_INIT, None, ALU.add)
            for h in range(H):
                for m in range(2):
                    i = 2 * h + m
                    b = bank(f"sc{h}{m}")
                    at, _w = CONST["bias"]
                    tt(att[:, m, :], b[:, 0:384], cst[:, at + h * 384:at + (h + 1) * 384], ALU.add)
                    free()
                    for q, (lo, hi) in enumerate(((0, P), (P, 3 * P))):
                        do(dve.tensor_reduce(sv("nm", 2 * i + q, 2 * i + q + 1), att[:, m, lo:hi], AX, ALU.max,
                                             negate=True))
                    dve.nop().then_inc(S("s_ready"), 1)
                dve.wait_ge(S("p_ready"), 4 * h + 4)
                do(dve.reciprocal(sv("r", 4 * h, 4 * h + 4), sv("l", 4 * h, 4 * h + 4)))
                ts(sv("r", 4 * h + 2, 4 * h + 4), sv("r", 4 * h + 2, 4 * h + 4), sv("lam", 4, 5), None, ALU.mult)
                for q, (lo, hi) in enumerate(((0, P), (P, 3 * P))):
                    r0, r1 = sv("r", 4 * h + q, 4 * h + q + 1), sv("r", 4 * h + 2 + q, 4 * h + 3 + q)
                    ts(att[:, 0, lo:hi], att[:, 0, lo:hi], r0, None, ALU.mult)
                    stt(pr(h)[:, lo:hi], att[:, 1, lo:hi], r1, att[:, 0, lo:hi], ALU.mult, ALU.add)
                dve.nop().then_inc(S("pd_ready"), 1)
            for h in range(H):
                copy(pr(h), bank(f"pt{h}")[:, 0:384])
                free()
            for h in range(H):
                copy(OB[:, h, 0:TP], bank(f"ob{h}")[:, 0:TP])
                free()
            for b in range(NS):
                q = bank(f"qb{b}")
                dve.wait_ge(S(f"k{b % 2}_loaded"), 32 * (b // 2 + 1))
                tt(prod, kpg[:, b % 2, :, :], q[:, :].unsqueeze(1).to_broadcast([P, NPG, W]), ALU.mult)
                free()
                do(dve.tensor_reduce(sS[:, :, 8 * b:8 * b + 8], prod.rearrange("p g (r d) -> p g r d", d=64),
                                     AX, ALU.add))
                dve.nop().then_inc(S("k_used"), 1)
            tt(self_prod, QT[:, :, TP:T].rearrange("p h b -> p b h"), KT_[:, :, TP:T].rearrange("p h b -> p b h"), ALU.mult)
            for m in range(2):
                ts(self_lhs4[:, :, :, m], self_prod, C("maps")[:, m:m + 1], None, ALU.mult)
            dve.nop().then_inc(S("self_ready"), 1)
            tt(sP, bank("ss")[0:64, 0:PAST + 1], C("sbias", 64), ALU.add)
            free()
            do(dve.tensor_reduce(sv("snm", rows=64), sP, AX, ALU.max, negate=True))
            dve.nop().then_inc(S("ss_ready"), 1)
            dve.wait_ge(S("sp_ready"), 1)
            do(dve.reciprocal(sv("sr", rows=64), sv("sl", rows=64)))
            lamc = C("lamc", 64)
            stt(sv("coef", rows=64), lamc[:, 1:2], sv("lam", 4, 5, 64), lamc[:, 0:1], ALU.mult, ALU.add)
            tt(sv("sr", rows=64), sv("sr", rows=64), sv("coef", rows=64), ALU.mult)
            ts(sC, C("pair", 64), sv("sr", rows=64), None, ALU.mult)
            copy(sPb, sP[:, PAST:PAST + 1].to_broadcast([64, P]))
            dve.nop().then_inc(S("pair_ready"), 1)
            copy(sD, bank("pd")[:, 0:96])
            free()
            dve.wait_ge(S("v_used"), NS)
            tt(OB[:, :, TP:T], sv("vbT").rearrange("p (h b) -> p h b", h=H),
               sD[:, 64:96].rearrange("p (b h) -> p h b", h=H), ALU.mult)
            tt(OB[:, :, TP:T], OB[:, :, TP:T], PB[4][:, 64:64 + H * NS].rearrange("p (h b) -> p h b", h=H), ALU.add)
            dve.nop().then_inc(S("oab_ready"), 1)
            ts(sv("gsl"), VT[:, VGB:VGB + 1], 1.0 - LAM_INIT, None, ALU.mult)
            for xname, OT, OTf in (("a", OA, OAf), ("b", OB, OBf)):
                for i in range(3):
                    cols = slice(i * 352, (i + 1) * 352)
                    ts(GCf[:, cols], bank(f"n{xname}{i}")[:, 0:352], 1.0 / DV, None, ALU.mult)
                    free()
                dve.nop().then_inc(S("ms_ready"), 1)
                dve.wait_ge(S("hrms_ready"), 1 if xname == "a" else 2)
                do(dve.reciprocal(GCf, GCf))
                for h in range(H):
                    g = VT[:, VGA + h:VGA + h + 1] if xname == "a" else sv("gsl")
                    stt(OT[:, h, :], OT[:, h, :], g, GC[:, h, :], ALU.mult, ALU.mult)
                if xname == "a":
                    tt(OT[:, :, :], OT[:, :, :], agT[:, :, :], ALU.mult)
                dve.nop().then_inc(S("oF_ready"), 1)
            for s in range(KC):
                dve.wait_ge(S("merge_full"), s + 1)
                tt(gaT[:, s, :], gaT[:, s, :], PB[2 * (s % 2)][:, 0:T], ALU.mult)
                tt(gbT[:, s, :], gbT[:, s, :], PB[2 * (s % 2) + 1][:, 0:T], ALU.mult)
                tt(gaT[:, s, :], gaT[:, s, :], gbT[:, s, :], ALU.add, "merge_free")

            def spread_rows(kind):
                for who, i, n in (("p", 0, P), ("s", 1, NS)):
                    for half in range(2):
                        copy(G[0:n, i, half * 512:(half + 1) * 512], bank(f"{kind}{who}{half}")[0:n, :])
                        free()

            spread_rows("g1")
            for c in range(NCH):
                n = rows_of[c]
                dve.wait_ge(S("y2_ready"), 2 * c + 2)
                tt(sv("rs", c, c + 1, n), sv("y2", 2 * c, 2 * c + 1, n), sv("y2", 2 * c + 1, 2 * c + 2, n), ALU.add,
                   "y2_summed")
                dve.wait_ge(S("yrms_ready"), c + 1)
                do(dve.reciprocal(sv("rs", c, c + 1, n), sv("rs", c, c + 1, n)))
                for i in range(2):
                    cols = slice(i * 512, (i + 1) * 512)
                    stt(xn[0:n, c, cols], PB[2 * (c % 2) + i][0:n, :], sv("rs", c, c + 1, n),
                        G[0:n, c // 2, cols], ALU.mult, ALU.mult)
                    tt(x[0:n, c, cols], x[0:n, c, cols], xn[0:n, c, cols], ALU.add)
                dve.nop().then_inc(S("yo_free"), 1)
                dve.nop().then_inc(S("x1_ready"), 1)
            dve.wait_ge(S("rms_ready"), 2)
            do(dve.reciprocal(sv("rs"), sv("rs")))
            for c in range(NCH):
                n = rows_of[c]
                ts(xn[0:n, c, :], x[0:n, c, :], sv("rs", c, c + 1, n), None, ALU.mult)
            dve.nop().then_inc(S("xn2_ready"), 1)
            modulate("h2t", A2, SH2)
            do(dve.memset(xn[:, 2, :], 0.0))
            for c in range(NCH):
                n = rows_of[c]
                for i in range(2):
                    copy(xn[0:n, c, i * 512:(i + 1) * 512], bank(f"h2r{c}{i}")[0:n, :])
                    free()
            do(dve.memset(vaf[:, 0:480], 0.0))
            for c in range(NCH):
                n = rows_of[c]
                tt(lg[0:n, c, :], bank(f"rt{c}")[0:n, 0:E], br[0:n, :], ALU.add)
                free()
                do(dve.max(sv("top", 8 * c, 8 * c + 8, n), lg[0:n, c, :]))
                ts(sv("gr", c, c + 1, n), sv("top", 8 * c, 8 * c + 1, n), -1.0, None, ALU.mult)
                dve.nop().then_inc(S("top_ready"), 1)
                do(dve.max_index(sv("idx", 8 * c, 8 * c + 8, n).bitcast(U32), sv("top", 8 * c, 8 * c + 8, n), lg[0:n, c, :]))
                copy(sv("idf", 8 * c, 8 * c + 8, n), sv("idx", 8 * c, 8 * c + 8, n).bitcast(U32))
                tt(onehot[0:n, c, :, :], C("iota_e", n).unsqueeze(1).to_broadcast([n, TOPK, E]),
                   sv("idf", 8 * c, 8 * c + 4, n).unsqueeze(2).to_broadcast([n, TOPK, E]), ALU.is_equal)
                do(dve.tensor_reduce(mask[0:n, c, :], onehot[0:n, c, :, :].rearrange("p k e -> p e k"), AX, ALU.add))
            dve.nop().then_inc(S("mask_ready"), 1)
            b = bank("pos")
            tot = b[:, NCH * E:(NCH + 1) * E]
            ts(sv("nb"), tot, float(M), 1.0, ALU.is_gt, ALU.add)
            for i in range(2, (T - 1) // M + 1):
                stt(sv("nb"), tot, float(i * M), sv("nb"), ALU.is_gt, ALU.add)
            do(dve.tensor_tensor_scan(sv("incl"), C("ones")[:, 0:E], sv("nb"), 0.0, ALU.mult, ALU.add))
            do(dve.memset(tab[0:1, :], 0))
            copy(tab[0:1, 1:E + 1], sv("incl", rows=1))
            do(dve.memset(used_tab[0:1, :], 0))
            ts(used_tab[0:1, 1:E], sv("incl", 0, E - 1, 1), -1.0, 12.0, ALU.add, ALU.mult)
            dve.nop().then_inc(S("tab_ready"), 1)
            tt(sv("cmp"), sv("incl"), sv("nb"), ALU.subtract)
            for c in range(NCH):
                n = rows_of[c]
                stt(lg[:, c, :], sv("cmp"), float(M), b[:, c * E:(c + 1) * E], ALU.mult, ALU.add)
                tt(eqt[:, 0:TOPK * E].rearrange("p (k e) -> p k e", k=TOPK), onehot[:, c, :, :],
                   lg[:, c, :].unsqueeze(1).to_broadcast([P, TOPK, E]), ALU.mult)
                do(dve.tensor_reduce(sv("g", 4 * c, 4 * c + 4, n),
                                     eqt[0:n, 0:TOPK * E].rearrange("p (k e) -> p k e", k=TOPK), AX, ALU.add))
            free()
            copy(sv("grel"), sv("g"))
            copy(gint[:, :], sv("g"))
            dve.wait_ge(S("ge_ready"), 3)
            for c in range(NCH):
                n = rows_of[c]
                do(dve.reciprocal(sv("gs", c, c + 1, n), sv("gs", c, c + 1, n)))
                ts(sv("ge", 4 * c, 4 * c + 4, n), sv("ge", 4 * c, 4 * c + 4, n), sv("gs", c, c + 1, n), None, ALU.mult)
            spread_rows("g2")

            iota = C("iota_slot").unsqueeze(1).to_broadcast([P, NCH * TOPK, M])
            eq3 = eqt.rearrange("p (g m) -> p g m", m=M)
            g3 = sv("grel").unsqueeze(2).to_broadcast([P, NCH * TOPK, M])
            eq_sum = eqt.rearrange("p (c k m) -> p c m k", c=NCH, k=TOPK)
            P3 = mo["Pm"].rearrange("p (c m) -> p c m", c=NCH)
            do(dve.tensor_tensor(eq3, iota, g3, ALU.is_equal))
            dve.tensor_reduce(P3, eq_sum, AX, ALU.add).then_inc(S("P_ready"), 1)
            dve.wait_ge(S("P_ready"), 1)
            nblocks = dve.value_load(tab[0:1, E:E + 1], min_val=1, max_val=MAXB)
            with dve.Fori(0, nblocks) as b:
                dve.tensor_scalar(sv("grel"), sv("grel"), float(-M), None, ALU.add).then_inc(S("grel_moved"), 1)
                dve.wait_ge(S("grel_moved"), b + 1)
                dve.tensor_tensor(eq3, iota, g3, ALU.is_equal).then_inc(S("eq_ready"), 1)
                dve.wait_ge(S("eq_ready"), b + 1)
                dve.wait_ge(S("gathered"), b + 1)
                dve.tensor_reduce(P3, eq_sum, AX, ALU.add).then_inc(S("P_ready"), 1)
                dve.wait_ge(S("gu_done"), b + 1)
                dve.wait_ge(S("P_ready"), b + 2)
                dve.tensor_scalar(mo["glu"], PB[0][:, :], LIMIT, None, ALU.min).then_inc(S("glu_ready"), 1)
                dve.tensor_scalar(mo["lin"], PB[1][:, :], LIMIT, -LIMIT, ALU.min, ALU.max).then_inc(S("gu_free"), 1)
                dve.wait_ge(S("glu_ready"), b + 1)
                dve.wait_ge(S("gu_free"), b + 1)
                dve.scalar_tensor_tensor(mo["lin"], mo["lin"], 1.0, mo["glu"], ALU.add, ALU.mult).then_inc(S("lg_ready"), 1)
                dve.wait_ge(S("lg_ready"), b + 1)
                dve.wait_ge(S("sig_ready"), b + 1)
                dve.tensor_tensor(mo["actm"], mo["lin"], mo["sig"], ALU.mult).then_inc(S("act_ready"), 1)
            for c in range(NCH):
                n = rows_of[c]
                for k in range(TOPK):
                    i = c * TOPK + k
                    src = ring[0:n, i * D:(i + 1) * D] if i < 8 else late[0:n, (i - 8) * D:(i - 7) * D]
                    dve.wait_ge(S(f"rows{i}_loaded"), 16)
                    gate = sv("ge", i, i + 1, n)
                    if k == 0:
                        ts(xn[0:n, c, :], src, gate, None, ALU.mult)
                    else:
                        stt(xn[0:n, c, :], src, gate, xn[0:n, c, :], ALU.mult, ALU.add)
                dve.nop().then_inc(S("m_ready"), 1)
                dve.wait_ge(S("rms_ready"), 3 + c)
                do(dve.reciprocal(sv("rs", c, c + 1, n), sv("rs", c, c + 1, n)))
                stt(xn[0:n, c, :], xn[0:n, c, :], sv("rs", c, c + 1, n), G[0:n, c // 2, :], ALU.mult, ALU.mult)
                tt(xn[0:n, c, :], xn[0:n, c, :], x[0:n, c, :], ALU.add)
                dve.nop().then_inc(S("final_ready"), 1)


_INS = ["x_prompt", "x_sample", "cache_k", "cache_v", "state_hgrn", "page_table", "c_prompt", "c_sample",
        "w_mod", "b_mod", "g_pre_mix", "g_post_mix", "g_pre_ffn", "g_post_ffn", "w_in", "hgrn_lb", "g_hgrn",
        "lam_q1", "lam_k1", "lam_q2", "lam_k2", "g_subln", "w_proj_a", "w_proj_b", "w_out",
        "w_router", "b_router", "w_gate_up", "b_gate_up", "w_down", "b_down"]
_OUTS = [(1, TP, D), (NS, 1, D), (1, 1, TP, H, DV), (1, 1, TP, H, DV), (1, 1, H, P, DV),
         (1, NS, 1, H, DV), (1, NS, 1, H, DV), (1, NS, H, P, DV)]


def kernel(**inputs):
    import concourse.bacc as bacc
    from concourse.bass_utils import run_bass_kernel_spmd

    nc = bacc.Bacc("TRN2", target_bir_lowering=False, num_devices=1)
    arrays, aps = {}, {}
    given = {n: np.ascontiguousarray(inputs[n]) for n in _INS}
    given["consts"] = constants()
    for name, v in given.items():
        arrays[f"in_{name}"] = v
        aps[name] = nc.dram_tensor(f"in_{name}", v.shape, mybir.dt.from_np(v.dtype), kind="ExternalInput").ap()
    outs = [nc.dram_tensor(f"out_{i}", s, F32, kind="ExternalOutput").ap() for i, s in enumerate(_OUTS)]
    build(nc, aps, outs)
    r = run_bass_kernel_spmd(nc, [arrays], core_ids=[0])
    return tuple(r.results[0][f"out_{i}"] for i in range(len(_OUTS)))
```

```python
from contextlib import ExitStack

import numpy as np

import concourse.bass as bass
from concourse import mybir

F32 = mybir.dt.float32
BF16 = mybir.dt.bfloat16
I32 = mybir.dt.int32
U32 = mybir.dt.uint32
ALU = mybir.AluOpType
ACT = mybir.ActivationFunctionType
AX = mybir.AxisListType.X

P = 128
D = 1024
KC = D // P
TP = 256
NS = 8
T = TP + NS
NCH = 3
H = 4
DV = 128
W = H * DV
CHUNK = 64
NHC = TP // CHUNK
PAGE = 128
NPG = 2
PAST = NPG * PAGE
E = 32
TOPK = 4
M = 64
MAXB = E + T * TOPK // M
LIMIT = 7.0
ALPHA = 1.702
EPS = 1e-6
LAM_INIT = 0.2
NEG = -1e30
SLOT = 2048
D_IN = 5632

CONST_WIDTHS = [("ident", 128), ("ones", 128), ("tri", 128), ("iota_slot", M), ("iota_e", E),
                ("causal", 128), ("bias", H * 384), ("scan", T), ("sbias", PAST + 1), ("pair", 32),
                ("selp", 128), ("sels", NS), ("maps", 2), ("lamc", 2), ("onehot_e", E)]
CONST = {}
_at = 0
for _n, _w in CONST_WIDTHS:
    CONST[_n] = (_at, _w)
    _at += _w
NCONST = _at


def constants():
    c = np.zeros((P, NCONST), np.float32)

    def put(name, a):
        at, w = CONST[name]
        c[: a.shape[0], at:at + w] = a

    p = np.arange(P)
    put("ident", np.eye(P))
    put("ones", np.ones((P, P)))
    put("tri", (p[:, None] < p[None, :]).astype(np.float32))
    put("iota_slot", np.tile(np.arange(M), (P, 1)))
    put("iota_e", np.tile(np.arange(E), (P, 1)))
    put("causal", ((p[:, None] // CHUNK == p[None, :] // CHUNK) & (p[:, None] <= p[None, :])))
    slopes = 2.0 ** (-8.0 * np.arange(1, H + 1) / H)
    bias = np.zeros((P, H, 384))
    for h in range(H):
        for lo, q0, n in ((0, 0, 128), (128, 128, 256)):
            dist = (q0 + p)[:, None] - np.arange(n)[None, :]
            bias[:, h, lo:lo + n] = np.where(dist >= 0, -slopes[h] * dist, NEG)
    put("bias", bias.reshape(P, -1))
    put("scan", np.tile((np.arange(T) % CHUNK != 0) & (np.arange(T) < TP), (P, 1)))
    r = np.arange(64)
    put("sbias", -slopes[(r // 2) % H][:, None] * (PAST - np.arange(PAST + 1))[None, :])
    put("pair", (r[:, None] // 2 == np.arange(32)[None, :]).astype(np.float32))
    put("selp", np.repeat((p % 32 == 0)[:, None], P, 1).astype(np.float32))
    put("sels", (p[:, None] % 32 == 1 + np.arange(NS)[None, :]).astype(np.float32))
    put("maps", np.stack([p < 64, p >= 64], 1).astype(np.float32))
    put("lamc", np.stack([p % 2 == 0, p % 2 == 1], 1).astype(np.float32))
    put("onehot_e", (p[:, None] % E == np.arange(E)[None, :]).astype(np.float32))
    return c


IN_ORDER = [4, 5, 6, 0, 1, 2, 3, 7, 8, 9, 10]
IN_NAMES = {0: [f"aq{j}" for j in range(4)], 1: [f"af{j}" for j in range(4)], 2: ["va0", "va1", "vas"],
            3: [f"ag{j}" for j in range(4)], 4: [f"bq{j}" for j in range(4)],
            5: [f"bk{j}" for j in range(4)], 6: ["vb0", "vb1", "vbs"],
            7: [f"ga{j}" for j in range(4)], 8: [f"ga{j}" for j in range(4, 8)],
            9: [f"gb{j}" for j in range(4)], 10: [f"gb{j}" for j in range(4, 8)]}
UNITS = [("mod", 0, k) for k in range(KC)]
_mods = [("mod", g, k) for g in (1, 2) for k in range(KC)]
for _u in IN_ORDER:
    for _half in range(2):
        UNITS.append(("in", _u, _half))
        UNITS += _mods[:2]
        _mods = _mods[2:]
UNITS += [("pb", 0), ("pb", 1), ("pa", 0), ("pa", 1)] + [("wo", q) for q in range(4)]
UNIT_AT = {u: n for n, u in enumerate(UNITS)}

AUX_ORDER = ["vt", "mt0"] + [f"xt{k}" for k in range(KC)] + """
    qs tok0 tok1 toks qb0 qb1 qb2 qb3 vbs sc00 sc01 sc10 sc11 sc20 sc21 sc30 sc31
    pt0 pt1 qb4 pt2 qb5 pt3 qb6 ob0 qb7 ob1 ss ob2 ob3 kt0 kt1 pd as0 as1
    kv0 vas kv1 kks kv2 ou00 ou01 kv3 mt1 ou10 ou11 oa0 oa1 oa2 oa3 ou20 ou21 ou30 ou31 mt2
    nb0 nb1 nb2 na0 na1 na2 g1p0 g1p1 g1s0 g1s1""".split()
AUX_ORDER += ([f"h2t{k}" for k in range(KC)] + [f"h2r{c}{i}" for c in range(NCH) for i in range(2)]
              + ["rt0", "rt1", "rt2", "pos", "g2p0", "g2p1", "g2s0", "g2s1"])
AUX = {n: i for i, n in enumerate(AUX_ORDER)}
PROJ_ORDER = [n for u in IN_ORDER for n in IN_NAMES[u]]
PROJ = {n: i for i, n in enumerate(PROJ_ORDER)}
NPROJ = len(PROJ_ORDER)


def build(nc, a, o):
    ctx = ExitStack()
    with ctx:
        def sb(name, shape, dt=F32):
            return ctx.enter_context(nc.sbuf_tensor(name, shape, dt))

        sems = {}

        def S(name):
            if name not in sems:
                sems[name] = ctx.enter_context(nc.semaphore(name))
            return sems[name]

        ring = sb("ring", [P, 4 * SLOT])
        late = sb("late", [P, 8 * SLOT])
        cst = sb("cst", [P, NCONST])
        x = sb("x", [P, NCH, D])
        wide = sb("wide", [P, NCH * D])
        hT = sb("hT", [P, KC, T])
        mod = sb("mod", [P, 3, 512])
        gpost = sb("gpost", [P, 512])
        G = sb("G", [P, 2, D])
        va = sb("va", [P, 2, W])
        vas = sb("vas", [NS, W])
        vb = sb("vb", [P, 2, W])
        vbs = sb("vbs", [NS, W])
        gates = sb("gates", [P, 2 * KC * T])
        agT = sb("agT", [P, H, T])
        att_even = sb("att", [P, 2, 384])
        tok = sb("tok", [P, W])
        biases = sb("biases", [96, 3 * D], BF16)
        sel = sb("sel", [96, M], BF16)
        small = sb("small", [P, 640])
        A1 = sb("A1", [P, KC, 9])
        SH1 = sb("SH1", [P, KC, 9])
        A2 = sb("A2", [P, KC, 9])
        SH2 = sb("SH2", [P, KC, 9])
        gint = sb("gint", [P, NCH * TOPK], I32)
        tab = sb("tab", [1, E + 1], I32)
        used_tab = sb("used_tab", [1, E], I32)
        pgt = sb("pgt", [1, NS * NPG], I32)
        ybuf = nc.dram_tensor("ybuf", (MAXB * M, D), F32, kind="Internal").ap()
        PB = [ctx.enter_context(nc.psum_tensor(f"PB{i}", [P, 512], F32)) for i in range(8)]

        def C(name, rows=P):
            at, w = CONST[name]
            return cst[0:rows, at:at + w]

        ident = C("ident")
        def late_tile(i, n=H * T):
            return late[:, i * H * T:i * H * T + n]

        AQ, FG, LN, GC, KK, KD, ET, OA, OB = (
            late_tile(i).rearrange("p (h t) -> p h t", h=H) for i in range(9))
        base = 9 * H * T
        SA = late[:, base:base + NHC * W].rearrange("p (c h v) -> p c h v", c=NHC, h=H)
        S0 = late[:, base + 2048:base + 4096].rearrange("p (s b v) -> p s b v", s=2, b=NS)
        QT = late[:, base + 4096:base + 4096 + H * T].rearrange("p (h t) -> p h t", h=H)
        at = base + 4096 + H * T
        KT_ = late[:, at:at + H * T].rearrange("p (h t) -> p h t", h=H)
        ET_rows = late_tile(6, 2 * W).rearrange("p (c n) -> p c n", c=2)
        A_rows = wide[:, 0:2 * W].rearrange("p (c h t) -> p c h t", c=2, h=H)

        def pr(h):
            return gates[:, h * 384:(h + 1) * 384]

        att_odd = gates[:, 4 * 384:6 * 384].rearrange("p (m n) -> p m n", m=2)
        att = [att_even, att_odd]
        qs_rows = vas
        hTf = hT[:, :, :].rearrange("p k t -> p (k t)")
        eps = sb("eps", [P, 1])
        VTs = sb("VTs", [P, 72])
        AQf, FGf, LNf, GCf, KKf, KDf, ETf, OAf, OBf = (late_tile(i) for i in range(9))
        krows = [LNf[:, 0:W], GCf[:, 0:W], GCf[0:NS, W:2 * W]]
        xn = wide[:, :].rearrange("p (c d) -> p c d", c=NCH)
        kpg = wide[:, 0:2048].rearrange("p (s g n) -> p s g n", s=2, g=NPG)
        vm = wide[0:NS, 2048:3072].rearrange("p (b v) -> p b v", b=NS)
        prod = wide[:, 2048:3072].rearrange("p (g n) -> p g n", g=NPG)
        vpg = G[:, :, :].rearrange("p s (g n) -> p s g n", g=NPG)
        gaT = gates[:, 0:KC * T].rearrange("p (s t) -> p s t", s=KC)
        gbT = gates[:, KC * T:2 * KC * T].rearrange("p (s t) -> p s t", s=KC)
        bias_f = gates[0:E, 0:3 * D]
        bias_t = gates[0:E, 3 * D:4 * D]
        wr = sb("wr", [P, KC, E])
        br = sb("br", [P, E])
        lamv = sb("lamv", [P, 4, 64])
        vrows = sb("vrows", [P, P])
        VT = sb("VT", [P, P])
        VC, VG1, VG2, VLB, VGA, VGB, NV = 0, 72, 80, 88, 96, 100, 101
        cT = sb("cT", [P, KC, 32])
        at += H * T
        assert at + 612 <= 8 * SLOT
        ssm = late[:, at:at + 612]
        sS = ssm[:, 0:128].rearrange("p (g r) -> p g r", g=NPG)
        sP = ssm[0:64, 128:128 + PAST + 1]
        sC = ssm[0:64, 388:420]
        sD = ssm[:, 420:516]
        self_prod = ssm[:, 516:548].rearrange("p (b h) -> p b h", b=NS)
        self_lhs = ssm[:, 548:612]
        self_lhs4 = self_lhs.rearrange("p (b h m) -> p b h m", b=NS, h=H)
        sPb = att_even[0:64, 0, 0:P]

        sm = {}
        at = 0
        for n, w in (("ssq", 3), ("rs", 3), ("lb", 12), ("omlb", 4), ("lam", 8), ("egl", 16), ("nm", 16),
                     ("l", 16), ("r", 16), ("snm", 1), ("sl", 1), ("sr", 1), ("top", 24), ("idx", 24),
                     ("idf", 24), ("ge", 12), ("gs", 3), ("gr", 3), ("g", 12), ("grel", 12),
                     ("nb", 32), ("incl", 32), ("cmp", 32), ("y2", 6), ("vaT", 32), ("vbT", 32),
                     ("osa", 32), ("osb", 32), ("gsl", 1), ("xs", 64), ("coef", 1), ("one", 1), ("big", 40)):
            sm[n] = (at, w)
            at += w
        assert at <= 640, at

        def sv(n, lo=0, hi=None, rows=P, r0=0):
            s, w = sm[n]
            return small[r0:rows, s + lo:s + (w if hi is None else hi)]

        mo = {}
        at = 0
        for n, w in (("glu", 512), ("lin", 512), ("sig", 512), ("actm", 512), ("xT", 512), ("actT", 512),
                     ("y", 512), ("Pm", NCH * M)):
            mo[n] = gates[:, at:at + w]
            at += w
        assert at <= 2 * KC * T
        eqt = att_even[:, :, :].rearrange("p m n -> p (m n)")
        vaf = va[:, :, :].rearrange("p c n -> p (c n)")
        onehot = vaf[:, 0:384].rearrange("p (c k e) -> p c k e", c=NCH, k=TOPK)
        mask = vaf[:, 384:480].rearrange("p (c e) -> p c e", c=NCH)
        lg = vaf[:, 480:576].rearrange("p (c e) -> p c e", c=NCH)

        def slot(i):
            return ring[:, i * SLOT:(i + 1) * SLOT] if i < 4 else late[:, (i - 4) * SLOT:(i - 3) * SLOT]

        def aux(name):
            return PB[5 + AUX[name] % 3]

        rows_of = [P, P, NS]

        def after_unit(n):
            u = UNITS[n]
            if u[0] == "mod":
                return "mod_used", KC * u[1] + u[2] + 1
            if u[0] == "in":
                names = IN_NAMES[u[1]]
                if u[2] == 1:
                    return "proj_full", PROJ[names[-1]] + 1
                return ("proj_full", PROJ[names[1]] + 1) if len(names) == 4 else ("tok_half", 1 if u[1] == 6 else 2)
            if u[0] in ("pb", "pa"):
                return "merge_full", (KC if u[0] == "pa" else 0) + 4 * (u[1] + 1)
            return "yo_full", NCH

        block = ctx.enter_context(nc.Block())

        @block.sync
        def _(sp):
            wmod = a["w_mod"][0].rearrange("(k p) n -> p k n", p=P)
            win = a["w_in"][0].rearrange("(k p) n -> p k n", p=P)
            for n, u in enumerate(UNITS):
                if n >= 4:
                    sem, value = after_unit(n - 4)
                    sp.wait_ge(S(sem), value)
                dst = slot(n % 4)
                if u[0] == "mod":
                    src = wmod[:, u[2], u[1] * 2048:(u[1] + 1) * 2048]
                elif u[0] == "in":
                    src = win[:, :, u[1] * 512 + u[2] * 256:u[1] * 512 + (u[2] + 1) * 256]
                    dst = dst.rearrange("p (k n) -> p k n", k=KC)
                elif u[0] in ("pa", "pb"):
                    w = a["w_proj_a" if u[0] == "pa" else "w_proj_b"][0].rearrange("(h p) n -> p h n", p=P)
                    src = w[:, :, u[1] * 512:(u[1] + 1) * 512]
                    dst = dst.rearrange("p (h n) -> p h n", h=H)
                else:
                    src = a["w_out"][0, u[1] * 256:(u[1] + 1) * 256, :].rearrange("(k p) n -> p k n", p=P)
                    dst = dst.rearrange("p (k n) -> p k n", k=2)
                sp.dma_start(dst, src).then_inc(S(f"piece{n % 4}_landed"), 16)

            def load_expert(e, u):
                one = slice(e, e + 1) if isinstance(e, int) else bass.ds(e, 1)
                if u < 8:
                    src = a["w_gate_up"][0, one, u * P:(u + 1) * P, :]
                    src = src.rearrange("e p n -> p (e n)")
                    dst = slot(u)
                else:
                    src = a["w_down"][0, one, (u - 8) * 2 * P:(u - 7) * 2 * P, :]
                    src = src.rearrange("e (k p) n -> p (e k) n", p=P)
                    dst = slot(u).rearrange("p (k n) -> p k n", k=2)
                sp.dma_start(dst, src).then_inc(S(f"w{u}_landed"), 16)

            sp.wait_ge(S("merge_full"), 2 * KC)
            sp.wait_ge(S("st_stored"), 16)
            for h in range(2):
                sp.wait_ge(S(f"s0_{h}_stored"), 32)
            for u in range(4, 12):
                load_expert(0, u)
            sp.wait_ge(S("yo_full"), NCH)
            for u in range(4):
                load_expert(0, u)
            sp.wait_ge(S("tab_ready"), 1)
            with sp.Fori(1, E) as e:
                before = sp.value_load(used_tab[0:1, bass.ds(e, 1)], min_val=0, max_val=12 * MAXB)
                for u in range(12):
                    sp.wait_ge(S("w_used"), before + (u + 1))
                    load_expert(e, u)

        @block.gpsimd
        def _(pool):
            pool.dma_start(pgt[0:1, :], a["page_table"].rearrange("(a b) n -> a (b n)", a=1)).then_inc(S("pg_loaded"), 16)
            for j in range(4):
                b = a["b_mod"]
                src = bass.AP(b.tensor, j * 512, [[0, 32], [2048, 3], [1, 512]])
                pool.dma_start(mod[32 * j:32 * j + 32, :, :], src).then_inc(S("bmod_loaded"), 16)
                g = a["g_post_mix"] if j < 2 else a["g_post_ffn"]
                src = bass.AP(g.tensor, (j % 2) * 512, [[0, 32], [1, 512]])
                pool.dma_start(gpost[32 * j:32 * j + 32, :], src).then_inc(S("gpost_loaded"), 16)
            pool.dma_start(bias_f[:, 0:2 * D], a["b_gate_up"][0]).then_inc(S("bias_loaded"), 16)
            pool.dma_start(bias_f[:, 2 * D:3 * D], a["b_down"][0]).then_inc(S("bias_loaded"), 16)
            for i, n in enumerate(("lam_q1", "lam_k1", "lam_q2", "lam_k2")):
                pool.dma_start(lamv[:, i, :], bass.AP(a[n].tensor, 0, [[0, P], [1, 64]])).then_inc(S("lam_loaded"), 16)
            pool.dma_start(wr[:, :, :], a["w_router"][0].rearrange("(k p) e -> p k e", p=P)).then_inc(S("wr_loaded"), 16)
            pool.dma_start(br[:, :], bass.AP(a["b_router"].tensor, 0, [[0, P], [1, E]])).then_inc(S("wr_loaded"), 16)

            st_in = a["state_hgrn"][0].rearrange("b h k v -> h k b v")
            st_out = o[7][0].rearrange("b h k v -> h k b v")
            for h in range(2):
                pool.dma_start(S0[:, h, :, :], st_in[h]).then_inc(S(f"s0_{h}_loaded"), 16)
            pool.wait_ge(S("tok_zero"), 1)
            reps = (MAXB - E) * M // P * 2
            pool.dma_start(ybuf[E * M:, :].rearrange("(p r) (h n) -> p (r h) n", p=P, n=W),
                           tok[:, :].unsqueeze(1).to_broadcast([P, reps, W])).then_inc(S("zero_stored"), 16)
            pool.wait_ge(S("pg_loaded"), 16)

            def pages(b, dst, cache, sem):
                for g in range(NPG):
                    page = pool.value_load(pgt[0:1, b * NPG + g:b * NPG + g + 1], min_val=0,
                                           max_val=a["cache_k"].shape[1] - 1)
                    src = a[cache][0, bass.ds(page, 1), :, :, :].rearrange("a p h n -> p (a h n)")
                    pool.dma_start(dst[:, b % 2, g, :], src).then_inc(S(f"{sem}{b % 2}_loaded"), 16)

            pool.wait_ge(S("hT_ready"), 1)
            for b in range(NS):
                if b >= 2:
                    pool.wait_ge(S("k_used"), b - 1)
                pages(b, kpg, "cache_k", "k")
            pages(0, vpg, "cache_v", "v")
            pages(1, vpg, "cache_v", "v")

            def next_values(lo):
                for b in (lo, lo + 1):
                    pool.wait_ge(S("v_used"), b - 1)
                    pages(b, vpg, "cache_v", "v")

            for h in range(H):
                pool.wait_ge(S("s0_ready"), h + 1)
                pool.dma_start(st_out[h], S0[:, h % 2, :, :]).then_inc(S(f"s0_{h % 2}_stored"), 16)
                if h == 0:
                    pool.wait_ge(S("state_ready"), 1)
                    pool.dma_start(o[4][0, 0].rearrange("h k v -> k h v"), SA[:, NHC - 1, :, :]).then_inc(S("st_stored"), 16)
                if h + 2 < H:
                    pool.wait_ge(S(f"s0_{h % 2}_stored"), 16)
                    pool.wait_ge(S("osa_used"), h + 1)
                    pool.dma_start(S0[:, h % 2, :, :], st_in[h + 2]).then_inc(S(f"s0_{h % 2}_loaded"), 16)
                if h >= 1:
                    next_values(2 * h)
            pool.wait_ge(S("tab_ready"), 1)
            pool.wait_ge(S("cst_loaded"), 16)
            at, _w = CONST["onehot_e"]
            pool.tensor_copy(sel[:, :], cst[0:96, at:at + 1].to_broadcast([96, M])).then_inc(S("sel_ready"), 1)
            with pool.Fori(1, E) as e:
                first = pool.value_load(tab[0:1, bass.ds(e, 1)], min_val=0, max_val=MAXB)
                pool.wait_ge(S("y_done"), first)
                pool.tensor_copy(sel[:, :], cst[0:96, bass.ds(e + at, 1)].to_broadcast([96, M])).then_inc(S("sel_ready"), 1)
            pool.wait_ge(S("y_all_stored"), 1)
            for c in range(NCH):
                n = rows_of[c]
                for k in range(TOPK):
                    i = c * TOPK + k
                    dst = ring[0:n, i * D:(i + 1) * D] if i < 8 else late[0:n, (i - 8) * D:(i - 7) * D]
                    pool.indirect_dma_start(
                        out=dst, out_offset=None, in_=ybuf,
                        in_offset=bass.IndirectOffsetOnAxis(ap=gint[0:n, i:i + 1].bitcast(U32), axis=0),
                    ).then_inc(S(f"rows{i}_loaded"), 16)

        @block.tensor
        def _(pe):
            def begin(name):
                if AUX[name] >= 3:
                    pe.wait_ge(S("aux_free"), AUX[name] - 2)
                return aux(name)

            def full(mm):
                mm.then_inc(S("aux_full"), 1)

            def unit(*key):
                n = UNIT_AT[key]
                pe.wait_ge(S(f"piece{n % 4}_landed"), 16 * (n // 4 + 1))
                return slot(n % 4)

            def tr(out, in_, n=P):
                return pe.transpose(out, in_, ident[0:n, 0:n])

            pe.wait_ge(S("small_loaded"), 16 * 8)
            full(tr(begin("vt")[:, 0:NV], vrows[0:NV, :], NV))

            def mod_part(g, k):
                if k == 0:
                    if g:
                        pe.wait_ge(S("mod_free"), g)
                    else:
                        pe.wait_ge(S("cT_ready"), 1)
                w = unit("mod", g, k)
                for j in range(4):
                    mm = pe.matmul(PB[4][32 * j:32 * j + 32, :], cT[:, k, :], w[:, j * 512:(j + 1) * 512],
                                   start=(k == 0), stop=(k == KC - 1))
                mm.then_inc(S("mod_used"), 1)

            mods = [(g, k) for g in (1, 2) for k in range(KC)]

            def two_mods():
                for _ in range(min(2, len(mods))):
                    mod_part(*mods.pop(0))

            def mod_cols(name, g):
                pe.wait_ge(S("mod_free"), g + 1)
                bank = begin(name)
                for q in range(4):
                    mm = tr(bank[:, q * P:(q + 1) * P], mod[:, g, q * P:(q + 1) * P])
                full(mm)

            def proj_bank(name):
                i = PROJ[name]
                if i >= 4:
                    pe.wait_ge(S("proj_free"), i - 3)
                return PB[i % 4]

            def in_T(u, *between):
                for j, name in enumerate(IN_NAMES[u]):
                    w = unit("in", u, j // 2)
                    bank = proj_bank(name)
                    for k in range(KC):
                        mm = pe.matmul(bank[:, 0:T], w[:, k * 256 + (j % 2) * P:k * 256 + (j % 2 + 1) * P], hT[:, k, :],
                                       start=(k == 0), stop=(k == KC - 1))
                    mm.then_inc(S("proj_full"), 1)
                    if j % 2:
                        two_mods()
                    if between:
                        for step in between[j]:
                            step[0](*step[1:])

            def in_tok(u, *between):
                names = IN_NAMES[u]
                banks = [proj_bank(n) for n in names]
                for half in range(2):
                    w = unit("in", u, half)
                    for c in range(2):
                        for k in range(KC):
                            mm = pe.matmul(banks[c][:, half * 256:(half + 1) * 256], hT[:, k, c * P:(c + 1) * P],
                                           w[:, k * 256:(k + 1) * 256], start=(k == 0), stop=(k == KC - 1))
                        if half:
                            mm.then_inc(S("proj_full"), 1)
                        for step in between[3 * half + c]:
                            step[0](*step[1:])
                    for j in range(2):
                        for k in range(KC):
                            mm = pe.matmul(banks[2][:, (2 * half + j) * NS:(2 * half + j + 1) * NS],
                                           w[:, k * 256 + j * P:k * 256 + (j + 1) * P],
                                           hT[:, k, TP:T], start=(k == 0), stop=(k == KC - 1))
                    mm.then_inc(S("proj_full" if half else "tok_half"), 1)
                    two_mods()
                    for step in between[3 * half + 2]:
                        step[0](*step[1:])

            def feature_major(prefix, ready, first):
                for k in range(KC):
                    if k == 0:
                        pe.wait_ge(S(ready), 1)
                    bank = begin(f"{prefix}{k}")
                    for c in range(NCH):
                        n = rows_of[c]
                        mm = tr(bank[:, c * P:c * P + n], first[0:n, c, k * P:(k + 1) * P], n)
                    full(mm)

            def keys_to_rows(c):
                bank = begin(f"kt{c}")
                pe.wait_ge(S("hg_k2"), 1)
                for h in range(H):
                    mm = tr(bank[:, h * P:(h + 1) * P], LN[:, h, c * P:(c + 1) * P])
                full(mm)

            def chunk_scores(c):
                bank = begin(f"as{c}")
                pe.wait_ge(S("hg_qk"), 1)
                for h in range(H):
                    mm = pe.matmul(bank[:, h * P:(h + 1) * P], KD[:, h, c * P:(c + 1) * P],
                                   AQ[:, h, c * P:(c + 1) * P], start=True, stop=True)
                full(mm)

            def chunk_update(c):
                bank = begin(f"kv{c}")
                pe.wait_ge(S("k2_rows"), 2)
                pe.wait_ge(S("proj_free"), PROJ["va1"] + 1)
                r = (c % 2) * CHUNK
                for h in range(H):
                    mm = pe.matmul(bank[:, h * P:(h + 1) * P],
                                   ET_rows[r:r + CHUNK, c // 2, h * P:(h + 1) * P],
                                   va[r:r + CHUNK, c // 2, h * P:(h + 1) * P], start=True, stop=True)
                full(mm)

            def out_a(h):
                bank = begin(f"oa{h}")
                pe.wait_ge(S("state_ready"), 1)
                for c in range(2):
                    mm = pe.matmul(bank[:, c * P:(c + 1) * P], va[:, c, h * P:(h + 1) * P],
                                   A_rows[:, c, h, :], start=True, stop=False)
                    for i in range(2):
                        g = 2 * c + i
                        if g:
                            mm = pe.matmul(bank[:, g * CHUNK:(g + 1) * CHUNK], SA[:, g - 1, h, :],
                                           AQ[:, h, g * CHUNK:(g + 1) * CHUNK], start=False, stop=(i == 1))
                full(mm)

            def rows_from(name, src, cols, n):
                bank = begin(name)
                pe.wait_ge(S("proj_free"), PROJ["bq3" if src is QT else "bk3"] + 1)
                if name == "kks":
                    pe.wait_ge(S("kk_ready"), 1)
                for h in range(H):
                    mm = tr(bank[0:n, h * P:(h + 1) * P], src[:, h, cols])
                full(mm)

            def value_rows(name, src):
                bank = begin(name)
                pe.wait_ge(S("proj_free"), PROJ[name] + 1)
                for h in range(H):
                    mm = tr(bank[0:NS, h * P:(h + 1) * P], sv(src, h * NS, (h + 1) * NS))
                full(mm)

            def outer(h):
                for b in range(2):
                    bank = begin(f"ou{h}{b}")
                    pe.wait_ge(S("aux_free"), AUX["kks"] + 1)
                    pe.wait_ge(S("vm_ready"), h + 1)
                    full(pe.matmul(bank[:, :], tok[0:NS, h * P:(h + 1) * P], vm[:, 4 * b:4 * b + 4, :],
                                   start=True, stop=True))

            def out_sample(h):
                pe.wait_ge(S("mod_free"), 3)
                pe.wait_ge(S("s0_ready"), h + 1)
                for b in range(NS):
                    mm = pe.matmul(PB[4][:, h * NS + b:h * NS + b + 1], S0[:, h % 2, b, :],
                                   AQ[:, h, TP + b:TP + b + 1], start=True, stop=True)
                mm.then_inc(S("osa_used"), 1)

            def scores(h, m):
                bank = begin(f"sc{h}{m}")
                pe.wait_ge(S("proj_free"), PROJ["bk3"] + 1)
                q, kk = QT[64 * m:64 * m + 64, h, :], KT_[64 * m:64 * m + 64, h, :]
                pe.matmul(bank[:, 0:P], q[:, 0:P], kk[:, 0:P], start=True, stop=True)
                full(pe.matmul(bank[:, P:3 * P], q[:, P:2 * P], kk[:, 0:2 * P], start=True, stop=True))

            def probs_T(h):
                bank = begin(f"pt{h}")
                pe.wait_ge(S("pd_ready"), h + 1)
                for i in range(3):
                    mm = tr(bank[:, i * P:(i + 1) * P], pr(h)[:, i * P:(i + 1) * P])
                full(mm)

            def out_b(h):
                bank = begin(f"ob{h}")
                pe.wait_ge(S("aux_free"), AUX[f"pt{h}"] + 1)
                pe.wait_ge(S("proj_free"), PROJ["vb1"] + 1)
                v = vb[:, :, h * P:(h + 1) * P]
                pe.matmul(bank[:, 0:P], v[:, 0, :], pr(h)[:, 0:P], start=True, stop=True)
                pe.matmul(bank[:, P:2 * P], v[:, 0, :], pr(h)[:, P:2 * P], start=True, stop=False)
                full(pe.matmul(bank[:, P:2 * P], v[:, 1, :], pr(h)[:, 2 * P:3 * P], start=False, stop=True))

            def query_rows(b):
                bank = begin(f"qb{b}")
                pe.wait_ge(S("aux_free"), AUX["qs"] + 1)
                full(pe.matmul(bank[:, :], ident[0:NS, b:b + 1].to_broadcast([NS, P]), qs_rows[0:NS, :],
                               start=True, stop=True))

            def sample_scores():
                bank = begin("ss")
                pe.wait_ge(S("cst_loaded"), 16)
                pe.wait_ge(S("self_ready"), 1)
                pe.wait_ge(S("k_used"), NS)
                for g in range(NPG):
                    tr(bank[0:64, g * P:(g + 1) * P], sS[:, g, :])
                full(pe.matmul(bank[0:64, PAST:PAST + 1], self_lhs, C("ones")[:, 0:1], start=True, stop=True))

            def sample_probs():
                bank = begin("pd")
                pe.wait_ge(S("pair_ready"), 1)
                for g in range(NPG):
                    pe.matmul(bank[:, g * 32:(g + 1) * 32], sP[:, g * P:(g + 1) * P], sC, start=True, stop=True)
                full(pe.matmul(bank[:, 64:96], sPb, sC, start=True, stop=True))

            def sample_values(b):
                pe.wait_ge(S("mod_free"), 3)
                pe.wait_ge(S("aux_free"), AUX["pd"] + 1)
                pe.wait_ge(S(f"v{b % 2}_loaded"), 32 * (b // 2 + 1))
                for h in range(H):
                    for g in range(NPG):
                        mm = pe.matmul(PB[4][:, 64 + h * NS + b:65 + h * NS + b], vpg[:, b % 2, g, h * P:(h + 1) * P],
                                       sD[:, g * 32 + b * H + h:g * 32 + b * H + h + 1],
                                       start=(g == 0), stop=(g == NPG - 1))
                mm.then_inc(S("v_used"), 1)

            for k in range(KC):
                mod_part(0, k)
            mod_cols("mt0", 0)
            feature_major("xt", "xn_ready", xn)
            pe.wait_ge(S("hT_ready"), 1)
            in_T(4)
            in_T(5)
            in_tok(6, [(rows_from, "qs", QT, slice(TP, T), NS)],
                   [(rows_from, "tok0", KT_, slice(0, P), P)],
                   [(rows_from, "tok1", KT_, slice(P, 2 * P), P)],
                   [(rows_from, "toks", KT_, slice(TP, T), NS), (query_rows, 0)],
                   [(query_rows, 1)], [(query_rows, 2)])
            in_T(0, [(query_rows, 3), (value_rows, "vbs", "vbT")], [(scores, 0, 0)], [(scores, 0, 1)], [(scores, 1, 0)])
            in_T(1, [(scores, 1, 1)], [(scores, 2, 0)], [(scores, 2, 1)], [(scores, 3, 0)])
            in_tok(2, [(scores, 3, 1)], [(probs_T, 0)], [(probs_T, 1)], [(query_rows, 4)], [(probs_T, 2)],
                   [(query_rows, 5)])
            in_T(3, [(probs_T, 3), (query_rows, 6)], [(out_b, 0), (query_rows, 7)], [(out_b, 1), (sample_scores,)],
                 [(out_b, 2), (out_b, 3)])
            in_T(7, [(keys_to_rows, 0), (keys_to_rows, 1)], [(sample_probs,)], [(chunk_scores, 0)], [(chunk_scores, 1)])
            in_T(8, [(chunk_update, 0), (value_rows, "vas", "vaT")],
                 [(chunk_update, 1), (rows_from, "kks", KK, slice(TP, T), NS)],
                 [(chunk_update, 2), (outer, 0)], [(chunk_update, 3), (mod_cols, "mt1", 1)])
            in_T(9, [(out_sample, 0), (outer, 1)], [(out_a, 0), (out_a, 1)],
                 [(out_sample, 1), (out_a, 2), (out_a, 3), (sample_values, 0), (sample_values, 1)],
                 [(outer, 2), (sample_values, 2), (sample_values, 3)])
            in_T(10, [(out_sample, 2), (outer, 3)], [(sample_values, 4), (sample_values, 5)],
                 [(out_sample, 3), (sample_values, 6), (sample_values, 7)], [(mod_cols, "mt2", 2)])
            for xname, sq, ready in (("b", KDf, "sqb_ready"), ("a", ETf, "sqa_ready")):
                pe.wait_ge(S(ready), 1)
                for i in range(3):
                    full(pe.matmul(begin(f"n{xname}{i}")[:, 0:352], C("ones"), sq[:, i * 352:(i + 1) * 352],
                                   start=True, stop=True))
            def branch(name, src, first):
                for s in range(KC):
                    w = unit(name, s // 4)
                    i = first + s
                    if i >= 4:
                        pe.wait_ge(S("merge_free"), i - 3)
                    for h in range(H):
                        mm = pe.matmul(PB[i % 4][:, 0:T], w[:, h * 512 + (s % 4) * P:h * 512 + (s % 4 + 1) * P],
                                       src[:, h, :], start=(h == 0), stop=(h == H - 1))
                    mm.then_inc(S("merge_full"), 1)

            pe.wait_ge(S("proj_free"), NPROJ)
            pe.wait_ge(S("oF_ready"), 1)
            branch("pb", OB, 0)
            def spread(kind, tile, j0):
                for who, sl, n in (("p", C("selp"), P), ("s", C("sels"), NS)):
                    for i in range(2):
                        j = j0 + i
                        mm = pe.matmul(begin(f"{kind}{who}{i}")[0:n, :], sl[32 * j:32 * j + 32, :],
                                       tile[32 * j:32 * j + 32, :], start=True, stop=True, tile_position=(32 * j, 0))
                        full(mm)
            pe.wait_ge(S("grow_ready"), 2)
            spread("g1", mod[:, 1, :], 0)
            pe.wait_ge(S("oF_ready"), 2)
            branch("pa", OA, KC)
            pe.wait_ge(S("merge_free"), 2 * KC)
            wo = [unit("wo", q) for q in range(4)]
            for c in range(NCH):
                n = rows_of[c]
                if c == 2:
                    pe.wait_ge(S("yo_free"), 1)
                for i in range(2):
                    for s in range(KC):
                        w = wo[s // 2]
                        mm = pe.matmul(PB[2 * (c % 2) + i][0:n, :], gaT[:, s, c * P:c * P + n],
                                       w[:, (s % 2) * D + i * 512:(s % 2) * D + (i + 1) * 512],
                                       start=(s == 0), stop=(s == KC - 1))
                mm.then_inc(S("yo_full"), 1)
            feature_major("h2t", "xn2_ready", xn)
            pe.wait_ge(S("hT_ready"), 2)
            for c in range(NCH):
                n = rows_of[c]
                for i in range(2):
                    bank = begin(f"h2r{c}{i}")
                    for k in range(4):
                        mm = tr(bank[0:n, k * P:(k + 1) * P], hT[:, 4 * i + k, c * P:c * P + n])
                    full(mm)
            for c in range(NCH):
                n = rows_of[c]
                bank = begin(f"rt{c}")
                if c == 0:
                    pe.wait_ge(S("wr_loaded"), 32)
                for k in range(KC):
                    mm = pe.matmul(bank[0:n, 0:E], hT[:, k, c * P:c * P + n], wr[:, k, :],
                                   start=(k == 0), stop=(k == KC - 1))
                full(mm)
            pe.wait_ge(S("mask_ready"), 1)
            bank = begin("pos")
            for c in range(NCH + 1):
                for b in range(min(c, NCH - 1) + 1):
                    mm = pe.matmul(bank[:, c * E:(c + 1) * E], C("tri") if b == c else C("ones"), mask[:, b, :],
                                   start=(b == 0), stop=(b == min(c, NCH - 1)))
            full(mm)
            spread("g2", mod[:, 2, :], 2)

            def gather():
                for k in range(KC):
                    for c in range(NCH):
                        mm = pe.matmul(PB[3][:, k * M:(k + 1) * M], xn[:, c, k * P:(k + 1) * P],
                                       mo["Pm"][:, c * M:(c + 1) * M], start=(c == 0), stop=(c == NCH - 1))
                mm.then_inc(S("gathered"), 1)

            pe.wait_ge(S("P_ready"), 1)
            gather()
            pe.wait_ge(S("tab_ready"), 1)
            with pe.Fori(0, E) as e:
                first = pe.value_load(tab[0:1, bass.ds(e, 1)], min_val=0, max_val=MAXB)
                last = pe.value_load(tab[0:1, bass.ds(e + 1, 1)], min_val=1, max_val=MAXB)
                with pe.Fori(first, last) as b:
                    pe.wait_ge(S("xT_ready"), b + 1)
                    for k in range(KC):
                        pe.wait_ge(S(f"w{k}_landed"), (e + 1) * 16)
                        for i in range(2):
                            for half in range(2):
                                mm = pe.matmul(PB[i][64 * half:64 * half + 64, :], mo["xT"][:, k * M:(k + 1) * M],
                                               slot(k)[:, i * D + half * 512:i * D + (half + 1) * 512],
                                               start=(k == 0), stop=False)
                        mm.then_inc(S("w_used"), 1)
                    pe.wait_ge(S("sel_ready"), e + 1)
                    for i in range(2):
                        for half in range(2):
                            mm = pe.matmul(PB[i][64 * half:64 * half + 64, :], sel[:, :],
                                           biases[:, i * D + half * 512:i * D + (half + 1) * 512],
                                           start=False, stop=True)
                    mm.then_inc(S("gu_done"), 1)
                    pe.wait_ge(S("P_ready"), b + 2)
                    gather()
                    pe.wait_ge(S("act_ready"), b + 1)
                    for q in range(4):
                        mm = tr(PB[4][:, q * P:(q + 1) * P], mo["actm"][:, q * P:(q + 1) * P])
                    mm.then_inc(S("actT_done"), 1)
                    pe.wait_ge(S("actT_ready"), b + 1)
                    for k in range(KC):
                        if k % 2 == 0:
                            pe.wait_ge(S(f"w{8 + k // 2}_landed"), (e + 1) * 16)
                        for half in range(2):
                            mm = pe.matmul(PB[2][64 * half:64 * half + 64, :],
                                           mo["actT"][:, (k % 4) * P + (k // 4) * M:(k % 4) * P + (k // 4) * M + M],
                                           slot(8 + k // 2)[:, (k % 2) * D + half * 512:(k % 2) * D + (half + 1) * 512],
                                           start=(k == 0), stop=False)
                        if k % 2:
                            mm.then_inc(S("w_used"), 1)
                    for half in range(2):
                        mm = pe.matmul(PB[2][64 * half:64 * half + 64, :], sel[:, :],
                                       biases[:, 2 * D + half * 512:2 * D + (half + 1) * 512], start=False, stop=True)
                    mm.then_inc(S("y_done"), 1)

        @block.scalar
        def _(act):
            chain = {}

            def do(ins, sem="act_link"):
                chain[sem] = chain.get(sem, 0) + 1
                ins.then_inc(S(sem), 1)
                act.wait_ge(S(sem), chain[sem])

            for dst, src in ((vrows[VC:VC + 8, :], a["c_prompt"].rearrange("a (k p) -> (a k) p", p=P)),
                             (vrows[VC + 8:VC + 72, :], a["c_sample"].rearrange("a (k p) -> (a k) p", p=P)),
                             (vrows[VG1:VG1 + 8, :], a["g_pre_mix"].rearrange("a (k p) -> (a k) p", p=P)),
                             (vrows[VG2:VG2 + 8, :], a["g_pre_ffn"].rearrange("a (k p) -> (a k) p", p=P)),
                             (vrows[VLB:VLB + 8, :], a["hgrn_lb"].rearrange("a (k p) -> (a k) p", p=P)),
                             (vrows[VGA:VGA + 4, :], a["g_hgrn"][0]),
                             (vrows[VGB:VGB + 1, :], a["g_subln"]),
                             (ident, a["consts"][:, 0:P])):
                act.dma_start(dst, src).then_inc(S("small_loaded"), 16)
            act.dma_start(x[:, 0:2, :], a["x_prompt"][0].rearrange("(c p) d -> p c d", p=P)).then_inc(S("x_loaded"), 16)
            act.dma_start(x[0:NS, 2, :], a["x_sample"][:, 0, :]).then_inc(S("x_loaded"), 16)
            act.dma_start(cst[:, P:], a["consts"][:, P:]).then_inc(S("cst_loaded"), 16)
            act.wait_ge(S("vt_ready"), 1)
            do(act.activation(VTs[:, 0:72], VT[:, 0:72], ACT.Sigmoid), "csig_ready")
            act.wait_ge(S("x_loaded"), 32)
            act.wait_ge(S("ssq_zero"), 1)
            for c in range(NCH):
                n = rows_of[c]
                do(act.activation(hTf[0:n, 0:D], x[0:n, c, :], ACT.Square,
                                  accum_out=sv("ssq", c, c + 1, n)), "ssq_ready")
            do(act.activation(sv("rs"), sv("ssq"), ACT.Sqrt, scale=1.0 / D, bias=eps[:, :]), "rms_ready")
            act.wait_ge(S("lbd_ready"), 1)
            do(act.activation(sv("lb", 4, 12), sv("lb", 4, 12), ACT.Exp), "lbe_ready")

            def bank(name):
                i = PROJ[name]
                act.wait_ge(S("proj_full"), i + 1)
                return PB[i % 4]

            def take(dst, name, j, func=ACT.Copy, **kw):
                do(act.activation(dst[:, j, :], bank(f"{name}{j % 8}")[:, 0:T], func, **kw), "proj_free")

            def prompt_exp(h, m):
                i = 2 * h + m
                act.wait_ge(S("s_ready"), i + 1)
                for q, (lo, hi) in enumerate(((0, P), (P, 3 * P))):
                    c = 2 * i + q
                    s = att[h % 2][:, m, lo:hi]
                    do(act.activation(s, s, ACT.Exp, bias=sv("nm", c, c + 1), accum_out=sv("l", c, c + 1)), "p_ready")

            def take_rows(name, dst, sample):
                for c in range(2):
                    do(act.activation(dst[:, c, :], bank(f"{name}{c}")[:, :], ACT.Copy), "proj_free")
                do(act.activation(sample, bank(f"{name}s")[:, 0:32], ACT.Copy), "proj_free")

            for j in range(H):
                take(QT, "bq", j, scale=0.125)
            act.wait_ge(S("lam_dots"), 1)
            do(act.activation(sv("lam", 2, 4), sv("lam", 0, 2), ACT.Exp), "lam_exp")
            for j in range(H):
                take(KT_, "bk", j)
            take_rows("vb", vb, sv("vbT"))
            act.dma_start(o[3][0, 0].rearrange("(c p) h n -> p c (h n)", p=P), vb[:, :, :]).then_inc(S("out_stored"), 16)
            kout = o[2][0, 0].rearrange("(c p) h n -> c p (h n)", p=P)
            for c in range(2):
                act.wait_ge(S("tok_ready"), c + 1)
                act.dma_start(kout[c], krows[c]).then_inc(S("tok_stored"), 16)
            act.wait_ge(S("tok_ready"), 3)
            act.dma_start(o[5][0, :, 0].rearrange("b h n -> b (h n)"), krows[2]).then_inc(S("tok_stored"), 16)
            take(AQ, "aq", 0)
            take(AQ, "aq", 1)
            act.wait_ge(S("vbs_ready"), 1)
            act.dma_start(o[6][0, :, 0].rearrange("b h n -> b (h n)"), vbs[:, :]).then_inc(S("out_stored"), 16)
            take(AQ, "aq", 2)
            prompt_exp(0, 0)
            take(AQ, "aq", 3)
            prompt_exp(0, 1)
            for j, (h, m) in enumerate(((1, 0), (1, 1), (2, 0), (2, 1))):
                take(FG, "af", j)
                prompt_exp(h, m)
            do(act.activation(FGf, FGf, ACT.Sigmoid), "fsig_ready")
            prompt_exp(3, 0)
            prompt_exp(3, 1)
            act.wait_ge(S("f_ready"), 1)
            act.wait_ge(S("tok_stored"), 16 * 3)
            do(act.activation(LNf, FGf, ACT.Ln), "ln_ready")
            act.wait_ge(S("gc_ready"), 1)
            do(act.activation(ETf, GCf, ACT.Exp))
            do(act.activation(KDf, GCf, ACT.Exp, scale=-1.0), "eg_ready")
            take_rows("va", va, sv("vaT"))
            act.wait_ge(S("gd_ready"), 1)
            do(act.activation(LN[:, :, 0:TP], LN[:, :, 0:TP], ACT.Exp))
            do(act.activation(sv("egl").rearrange("p (h c) -> p h c", h=H),
                              GC[:, :, CHUNK - 1:TP:CHUNK], ACT.Exp), "egl_ready")
            for j in range(H):
                take(agT, "ag", j)
            act.wait_ge(S("ss_ready"), 1)
            do(act.activation(sP, sP, ACT.Exp, bias=sv("snm", rows=64), accum_out=sv("sl", rows=64)), "sp_ready")
            do(act.activation(OAf, agT[:, :, :].rearrange("p h t -> p (h t)"), ACT.Sigmoid), "gsig_ready")
            act.wait_ge(S("aux_free"), AUX["ob3"] + 1)
            for j in range(KC):
                take(gaT, "ga", j, ACT.Sigmoid)
            for j in range(KC):
                take(gbT, "gb", j, ACT.Sigmoid)
            act.wait_ge(S("ob_ready"), 1)
            do(act.activation(KDf, OBf, ACT.Square), "sqb_ready")
            act.wait_ge(S("oa_ready"), 1)
            do(act.activation(ETf, OAf, ACT.Square), "sqa_ready")
            for i, ms in enumerate((GCf, LNf)):
                act.wait_ge(S("ms_ready"), i + 1)
                do(act.activation(ms, ms, ACT.Sqrt, bias=eps[:, :]), "hrms_ready")
            for c in range(NCH):
                n = rows_of[c]
                act.wait_ge(S("yo_full"), c + 1)
                for i in range(2):
                    do(act.activation(eqt[0:n, 0:512], PB[2 * (c % 2) + i][0:n, :], ACT.Square,
                                      accum_out=sv("y2", 2 * c + i, 2 * c + i + 1, n)), "y2_ready")
                act.wait_ge(S("y2_summed"), c + 1)
                do(act.activation(sv("rs", c, c + 1, n), sv("rs", c, c + 1, n), ACT.Sqrt, scale=1.0 / D,
                                  bias=eps[0:n, :]), "yrms_ready")
            for c in range(NCH):
                n = rows_of[c]
                act.wait_ge(S("x1_ready"), c + 1)
                do(act.activation(hTf[0:n, 0:D], x[0:n, c, :], ACT.Square,
                                  accum_out=sv("ssq", c, c + 1, n)), "ssq_ready")
            do(act.activation(sv("rs"), sv("ssq"), ACT.Sqrt, scale=1.0 / D, bias=eps[:, :]), "rms_ready")
            for c in range(NCH):
                n = rows_of[c]
                act.wait_ge(S("top_ready"), c + 1)
                do(act.activation(sv("ge", 4 * c, 4 * c + 4, n), sv("top", 8 * c, 8 * c + 4, n), ACT.Exp,
                                  bias=sv("gr", c, c + 1, n), accum_out=sv("gs", c, c + 1, n)), "ge_ready")
            act.wait_ge(S("gathered"), 1)
            act.activation(mo["xT"], PB[3][:, :], ACT.Copy).then_inc(S("xT_ready"), 1)
            act.wait_ge(S("tab_ready"), 1)
            nblocks = act.value_load(tab[0:1, E:E + 1], min_val=1, max_val=MAXB)
            with act.Fori(0, nblocks) as b:
                act.wait_ge(S("glu_ready"), b + 1)
                act.activation(mo["sig"], mo["glu"], ACT.Sigmoid, scale=ALPHA).then_inc(S("sig_ready"), 1)
                act.wait_ge(S("gathered"), b + 2)
                act.activation(mo["xT"], PB[3][:, :], ACT.Copy).then_inc(S("xT_ready"), 1)
                act.wait_ge(S("actT_done"), b + 1)
                act.activation(mo["actT"], PB[4][:, :], ACT.Copy).then_inc(S("actT_ready"), 1)
                act.wait_ge(S("y_done"), b + 1)
                act.wait_ge(S("y_stored"), b * 32)
                act.activation(mo["y"], PB[2][:, :], ACT.Copy).then_inc(S("y_free"), 1)
                act.wait_ge(S("y_free"), b + 1)
                for half in range(2):
                    act.dma_start(ybuf[bass.ds(b * M, M), half * 512:(half + 1) * 512],
                                  mo["y"][64 * half:64 * half + 64, :]).then_inc(S("y_stored"), 16)
            act.wait_ge(S("y_stored"), nblocks * 32)
            act.wait_ge(S("zero_stored"), 16)
            act.nop().then_inc(S("y_all_stored"), 1)
            for c in range(NCH):
                n = rows_of[c]
                act.wait_ge(S("m_ready"), c + 1)
                do(act.activation(hTf[0:n, 0:D], xn[0:n, c, :], ACT.Square, accum_out=sv("ssq", c, c + 1, n)),
                   "ssq_ready")
                do(act.activation(sv("rs", c, c + 1, n), sv("ssq", c, c + 1, n), ACT.Sqrt, scale=1.0 / D,
                                  bias=eps[0:n, :]), "rms_ready")
            for c in range(NCH):
                act.wait_ge(S("final_ready"), c + 1)
                if c < 2:
                    act.dma_start(o[0][0, c * P:(c + 1) * P, :], xn[:, c, :]).then_inc(S("out_stored"), 16)
                else:
                    act.dma_start(o[1][:, 0, :], xn[0:NS, c, :]).then_inc(S("out_stored"), 16)
            act.wait_ge(S("out_stored"), 16 * 5)
            act.wait_ge(S("tok_stored"), 16 * 3)
            act.wait_ge(S("st_stored"), 16)
            for h in range(2):
                act.wait_ge(S(f"s0_{h}_stored"), 32)

        @block.vector
        def _(dve):
            chain = {}

            def do(ins, sem="dve_link"):
                chain[sem] = chain.get(sem, 0) + 1
                ins.then_inc(S(sem), 1)
                dve.wait_ge(S(sem), chain[sem])

            def bank(name):
                dve.wait_ge(S("aux_full"), AUX[name] + 1)
                return aux(name)

            def ts(out, in_, s1, s2, op0, op1=None, sem="dve_link"):
                do(dve.tensor_scalar(out, in_, s1, s2, op0, op1) if op1 is not None
                   else dve.tensor_scalar(out, in_, s1, None, op0), sem)

            def tt(out, x0, x1, op, sem="dve_link"):
                do(dve.tensor_tensor(out, x0, x1, op), sem)

            def stt(out, x0, s, x1, op0, op1, sem="dve_link"):
                do(dve.scalar_tensor_tensor(out, x0, s, x1, op0, op1), sem)

            def copy(out, in_, sem="dve_link"):
                do(dve.tensor_copy(out, in_), sem)

            do(dve.memset(small[:, :], 0.0))
            do(dve.memset(eps[:, :], EPS), "ssq_zero")
            do(dve.memset(cT[:, :, :], 0.0))
            do(dve.memset(sv("g"), -1.0))
            do(dve.memset(tok[:, :], 0.0), "tok_zero")
            copy(VT[:, 0:NV], bank("vt")[:, 0:NV])
            dve.nop().then_inc(S("aux_free"), 1)
            dve.nop().then_inc(S("vt_ready"), 1)
            l0, l1 = VT[:, VLB:VLB + 4], VT[:, VLB + 4:VLB + 8]
            tt(sv("lb", 0, 4), l0, l1, ALU.max)
            tt(sv("lb", 4, 8), l0, sv("lb", 0, 4), ALU.subtract)
            tt(sv("lb", 8, 12), l1, sv("lb", 0, 4), ALU.subtract)
            dve.nop().then_inc(S("lbd_ready"), 1)
            dve.wait_ge(S("csig_ready"), 1)
            do(dve.tensor_tensor(cT[:, :, 0:9], VT[:, 0:72].rearrange("p (r k) -> p k r", r=9),
                                 VTs[:, 0:72].rearrange("p (r k) -> p k r", r=9), ALU.mult), "cT_ready")
            dve.wait_ge(S("rms_ready"), 1)
            do(dve.reciprocal(sv("rs"), sv("rs")))
            for c in range(NCH):
                n = rows_of[c]
                ts(xn[0:n, c, :], x[0:n, c, :], sv("rs", c, c + 1, n), None, ALU.mult)
            dve.nop().then_inc(S("xn_ready"), 1)
            def mod_rows(g):
                dve.wait_ge(S("mod_used"), KC * (g + 1))
                if g == 0:
                    dve.wait_ge(S("bmod_loaded"), 64)
                do(dve.tensor_tensor(mod[:, g, :], PB[4][:, :], mod[:, g, :], ALU.add), "mod_free")

            def scale_cols(A, b4, kind, gains):
                src = b4.rearrange("p (q j r) -> p j q r", q=4, j=4)[:, 2 * kind:2 * kind + 2, :, 0:9]
                for j in range(2):
                    g = VT[:, gains + 4 * j:gains + 4 * j + 4].unsqueeze(2).to_broadcast([P, 4, 9])
                    stt(A[:, 4 * j:4 * j + 4, :], src[:, j], 1.0, g, ALU.add, ALU.mult)

            def shift_cols(SH, b4, kind):
                src = b4.rearrange("p (q j r) -> p j q r", q=4, j=4)[:, 2 * kind:2 * kind + 2, :, 0:9]
                for j in range(2):
                    copy(SH[:, 4 * j:4 * j + 4, :], src[:, j])

            def free():
                dve.nop().then_inc(S("aux_free"), 1)

            def modulate(prefix, A, SH):
                for k in range(KC):
                    b = bank(f"{prefix}{k}")
                    ts(hT[:, k, 0:TP], b[:, 0:TP], A[:, k, 0:1], SH[:, k, 0:1], ALU.mult, ALU.add)
                    tt(hT[:, k, TP:T], b[:, TP:T], A[:, k, 1:9], ALU.mult)
                    free()
                tt(hT[:, :, TP:T], hT[:, :, TP:T], SH[:, :, 1:9], ALU.add)
                dve.nop().then_inc(S("hT_ready"), 1)

            mod_rows(0)
            b = bank("mt0")
            shift_cols(SH1, b, 0)
            scale_cols(A1, b, 1, VG1)
            free()
            modulate("xt", A1, SH1)
            dve.wait_ge(S("lbe_ready"), 1)
            tt(sv("lb", 0, 4), sv("lb", 4, 8), sv("lb", 8, 12), ALU.add)
            do(dve.reciprocal(sv("lb", 0, 4), sv("lb", 0, 4)))
            tt(sv("lb", 0, 4), sv("lb", 4, 8), sv("lb", 0, 4), ALU.mult)
            ts(sv("omlb"), sv("lb", 0, 4), -1.0, 1.0, ALU.mult, ALU.add)
            dve.wait_ge(S("lam_loaded"), 64)
            for i in range(2):
                tt(lamv[:, 2 * i, :], lamv[:, 2 * i, :], lamv[:, 2 * i + 1, :], ALU.mult)
                do(dve.tensor_reduce(sv("lam", i, i + 1), lamv[:, 2 * i, :], AX, ALU.add))
            dve.nop().then_inc(S("lam_dots"), 1)
            dve.wait_ge(S("bias_loaded"), 32)
            for i in range(3):
                cols = slice(i * D, (i + 1) * D)
                for part in range(3):
                    copy(biases[32 * part:32 * part + 32, cols], bias_f[:, cols])
                    if part < 2:
                        copy(bias_t, biases[32 * part:32 * part + 32, cols])
                        tt(bias_f[:, cols], bias_f[:, cols], bias_t, ALU.subtract)
            mod_rows(1)

            def rows_out(name, dst, ready=None):
                copy(dst, bank(name)[0:dst.shape[0], :])
                free()
                if ready:
                    dve.nop().then_inc(S(ready), 1)

            def query(b):
                q = bank(f"qb{b}")
                dve.wait_ge(S(f"k{b % 2}_loaded"), 32 * (b // 2 + 1))
                tt(prod, kpg[:, b % 2, :, :], q[:, :].unsqueeze(1).to_broadcast([P, NPG, W]), ALU.mult)
                free()
                do(dve.tensor_reduce(sS[:, :, 8 * b:8 * b + 8], prod.rearrange("p g (r d) -> p g r d", d=64),
                                     AX, ALU.add))
                dve.nop().then_inc(S("k_used"), 1)

            def biased(h, m):
                i = 2 * h + m
                b = bank(f"sc{h}{m}")
                at, _w = CONST["bias"]
                s = att[h % 2]
                tt(s[:, m, :], b[:, 0:384], cst[:, at + h * 384:at + (h + 1) * 384], ALU.add)
                free()
                for q, (lo, hi) in enumerate(((0, P), (P, 3 * P))):
                    do(dve.tensor_reduce(sv("nm", 2 * i + q, 2 * i + q + 1), s[:, m, lo:hi], AX, ALU.max, negate=True))
                dve.nop().then_inc(S("s_ready"), 1)

            def difference(h):
                s = att[h % 2]
                dve.wait_ge(S("p_ready"), 4 * h + 4)
                do(dve.reciprocal(sv("r", 4 * h, 4 * h + 4), sv("l", 4 * h, 4 * h + 4)))
                ts(sv("r", 4 * h + 2, 4 * h + 4), sv("r", 4 * h + 2, 4 * h + 4), sv("lam", 4, 5), None, ALU.mult)
                for q, (lo, hi) in enumerate(((0, P), (P, 3 * P))):
                    r0, r1 = sv("r", 4 * h + q, 4 * h + q + 1), sv("r", 4 * h + 2 + q, 4 * h + 3 + q)
                    ts(s[:, 0, lo:hi], s[:, 0, lo:hi], r0, None, ALU.mult)
                    stt(pr(h)[:, lo:hi], s[:, 1, lo:hi], r1, s[:, 0, lo:hi], ALU.mult, ALU.add)
                dve.nop().then_inc(S("pd_ready"), 1)

            def probs(h):
                copy(pr(h), bank(f"pt{h}")[:, 0:384])
                free()

            def out_b(h):
                copy(OB[:, h, 0:TP], bank(f"ob{h}")[:, 0:TP])
                free()

            def out_a(h):
                copy(OA[:, h, 0:TP], bank(f"oa{h}")[:, 0:TP])
                free()

            rows_out("qs", qs_rows[0:NS, :])
            rows_out("tok0", krows[0], "tok_ready")
            rows_out("tok1", krows[1], "tok_ready")
            rows_out("toks", krows[2], "tok_ready")
            for b in range(4):
                query(b)
            rows_out("vbs", vbs[:, :], "vbs_ready")
            dve.wait_ge(S("lam_exp"), 1)
            tt(sv("lam", 4, 5), sv("lam", 3, 4), sv("lam", 2, 3), ALU.subtract)
            ts(sv("lam", 4, 5), sv("lam", 4, 5), -LAM_INIT, None, ALU.add)
            dve.wait_ge(S("cst_loaded"), 16)
            biased(0, 0)
            biased(0, 1)
            biased(1, 0)
            difference(0)
            biased(1, 1)
            biased(2, 0)
            mod_rows(2)
            difference(1)
            biased(2, 1)
            biased(3, 0)
            difference(2)
            biased(3, 1)
            dve.wait_ge(S("fsig_ready"), 1)
            for h in range(H):
                ts(FG[:, h, :], FG[:, h, :], sv("omlb", h, h + 1), sv("lb", h, h + 1), ALU.mult, ALU.add)
            dve.nop().then_inc(S("f_ready"), 1)
            ts(KKf, FGf, -1.0, 1.0, ALU.mult, ALU.add, "kk_ready")
            probs(0)
            difference(3)
            dve.wait_ge(S("ln_ready"), 1)
            for h in range(H):
                do(dve.tensor_tensor_scan(GC[:, h, :], C("scan"), LN[:, h, :], 0.0, ALU.mult, ALU.add))
            dve.nop().then_inc(S("gc_ready"), 1)
            probs(1)
            for h in range(H):
                last = GC[:, h, CHUNK - 1:TP:CHUNK].unsqueeze(2).to_broadcast([P, NHC, CHUNK])
                tt(LN[:, h, 0:TP].rearrange("p (c t) -> p c t", c=NHC), last,
                   GC[:, h, 0:TP].rearrange("p (c t) -> p c t", c=NHC), ALU.subtract)
            dve.nop().then_inc(S("gd_ready"), 1)
            query(4)
            probs(2)
            query(5)
            dve.wait_ge(S("eg_ready"), 1)
            tt(AQ[:, :, 0:TP], AQ[:, :, 0:TP], ET[:, :, 0:TP], ALU.mult)
            tt(KDf, KDf, KKf, ALU.mult)
            dve.nop().then_inc(S("hg_qk"), 1)
            probs(3)
            query(6)
            out_b(0)
            query(7)
            do(dve.memset(wide[:, 0:2 * W], 0.0))
            tt(self_prod, QT[:, :, TP:T].rearrange("p h b -> p b h"), KT_[:, :, TP:T].rearrange("p h b -> p b h"), ALU.mult)
            for m in range(2):
                ts(self_lhs4[:, :, :, m], self_prod, C("maps")[:, m:m + 1], None, ALU.mult)
            dve.nop().then_inc(S("self_ready"), 1)
            out_b(1)
            tt(sP, bank("ss")[0:64, 0:PAST + 1], C("sbias", 64), ALU.add)
            free()
            do(dve.tensor_reduce(sv("snm", rows=64), sP, AX, ALU.max, negate=True))
            dve.nop().then_inc(S("ss_ready"), 1)
            dve.wait_ge(S("egl_ready"), 1)
            tt(LN[:, :, 0:TP], LN[:, :, 0:TP], KK[:, :, 0:TP], ALU.mult)
            dve.nop().then_inc(S("hg_k2"), 1)
            out_b(2)
            out_b(3)
            dve.wait_ge(S("sp_ready"), 1)
            do(dve.reciprocal(sv("sr", rows=64), sv("sl", rows=64)))
            lamc = C("lamc", 64)
            stt(sv("coef", rows=64), lamc[:, 1:2], sv("lam", 4, 5, 64), lamc[:, 0:1], ALU.mult, ALU.add)
            tt(sv("sr", rows=64), sv("sr", rows=64), sv("coef", rows=64), ALU.mult)
            ts(sC, C("pair", 64), sv("sr", rows=64), None, ALU.mult)
            copy(sPb, sP[:, PAST:PAST + 1].to_broadcast([64, P]))
            dve.nop().then_inc(S("pair_ready"), 1)
            for c in range(2):
                copy(ET_rows[:, c, :], bank(f"kt{c}")[:, :], "k2_rows")
                free()
            copy(sD, bank("pd")[:, 0:96])
            free()
            dve.wait_ge(S("gsig_ready"), 1)
            tt(agT[:, :, :], agT[:, :, :], OA[:, :, :], ALU.mult)
            for c in range(2):
                b = bank(f"as{c}")
                for h in range(H):
                    do(dve.copy_predicated(A_rows[:, c, h, :], C("causal").bitcast(U32), b[:, h * P:(h + 1) * P]))
                free()

            def chunk_state(c):
                b = bank(f"kv{c}")
                for h in range(H):
                    kv = b[:, h * P:(h + 1) * P]
                    if c == 0:
                        copy(SA[:, 0, h, :], kv)
                    else:
                        i = h * NHC + c
                        stt(SA[:, c, h, :], SA[:, c - 1, h, :], sv("egl", i, i + 1), kv, ALU.mult, ALU.add)
                free()

            def diagonal(h):
                tt(vm, vas[:, h * P:(h + 1) * P].unsqueeze(1).to_broadcast([NS, NS, P]),
                   ident[0:NS, 0:NS].unsqueeze(2).to_broadcast([NS, NS, P]), ALU.mult, "vm_ready")

            def sample_state(h):
                dve.wait_ge(S(f"s0_{h % 2}_loaded"), 16 * (h // 2 + 1))
                for b2 in range(2):
                    b = bank(f"ou{h}{b2}")
                    for i in range(4):
                        s = 4 * b2 + i
                        stt(S0[:, h % 2, s, :], S0[:, h % 2, s, :], FG[:, h, TP + s:TP + s + 1],
                            b[:, i * P:(i + 1) * P], ALU.mult, ALU.add)
                    free()
                dve.nop().then_inc(S("s0_ready"), 1)

            chunk_state(0)
            copy(vas[:, :], bank("vas")[0:NS, :])
            free()
            diagonal(0)
            chunk_state(1)
            dve.wait_ge(S("zero_stored"), 16)
            copy(tok[0:NS, :], bank("kks")[0:NS, :])
            free()
            chunk_state(2)
            sample_state(0)
            chunk_state(3)
            dve.nop().then_inc(S("state_ready"), 1)
            diagonal(1)
            shift_cols(SH2, bank("mt1"), 1)
            free()
            sample_state(1)
            diagonal(2)
            for h in range(H):
                out_a(h)
            sample_state(2)
            diagonal(3)
            sample_state(3)
            tt(OB[:, :, TP:T], sv("vbT").rearrange("p (h b) -> p h b", h=H),
               sD[:, 64:96].rearrange("p (b h) -> p h b", h=H), ALU.mult)
            dve.wait_ge(S("v_used"), NS)
            tt(OB[:, :, TP:T], OB[:, :, TP:T], PB[4][:, 64:64 + H * NS].rearrange("p (h b) -> p h b", h=H), ALU.add)
            dve.nop().then_inc(S("ob_ready"), 1)
            dve.wait_ge(S("osa_used"), H)
            copy(OA[:, :, TP:T], PB[4][:, 0:H * NS].rearrange("p (h b) -> p h b", h=H))
            dve.nop().then_inc(S("oa_ready"), 1)
            scale_cols(A2, bank("mt2"), 0, VG2)
            free()
            dve.wait_ge(S("gpost_loaded"), 64)
            tt(mod[0:64, 1, :], mod[0:64, 1, :], gpost[0:64, :], ALU.mult, "grow_ready")
            tt(mod[64:128, 2, :], mod[64:128, 2, :], gpost[64:128, :], ALU.mult, "grow_ready")
            ts(sv("gsl"), VT[:, VGB:VGB + 1], 1.0 - LAM_INIT, None, ALU.mult)
            for xname, OT, ms, msf in (("b", OB, GC, GCf), ("a", OA, LN, LNf)):
                for i in range(3):
                    cols = slice(i * 352, (i + 1) * 352)
                    ts(msf[:, cols], bank(f"n{xname}{i}")[:, 0:352], 1.0 / DV, None, ALU.mult)
                    free()
                dve.nop().then_inc(S("ms_ready"), 1)
                dve.wait_ge(S("hrms_ready"), 1 if xname == "b" else 2)
                do(dve.reciprocal(msf, msf))
                for h in range(H):
                    g = VT[:, VGA + h:VGA + h + 1] if xname == "a" else sv("gsl")
                    stt(OT[:, h, :], OT[:, h, :], g, ms[:, h, :], ALU.mult, ALU.mult)
                if xname == "a":
                    tt(OT[:, :, :], OT[:, :, :], agT[:, :, :], ALU.mult)
                dve.nop().then_inc(S("oF_ready"), 1)
            for s in range(KC):
                dve.wait_ge(S("merge_full"), s + 1)
                tt(gbT[:, s, :], gbT[:, s, :], PB[s % 4][:, 0:T], ALU.mult, "merge_free")

            def spread_rows(kind):
                for who, i, n in (("p", 0, P), ("s", 1, NS)):
                    for half in range(2):
                        copy(G[0:n, i, half * 512:(half + 1) * 512], bank(f"{kind}{who}{half}")[0:n, :])
                        free()

            spread_rows("g1")
            for s in range(KC):
                dve.wait_ge(S("merge_full"), KC + s + 1)
                tt(gaT[:, s, :], gaT[:, s, :], PB[s % 4][:, 0:T], ALU.mult)
                tt(gaT[:, s, :], gaT[:, s, :], gbT[:, s, :], ALU.add, "merge_free")

            for c in range(NCH):
                n = rows_of[c]
                dve.wait_ge(S("y2_ready"), 2 * c + 2)
                tt(sv("rs", c, c + 1, n), sv("y2", 2 * c, 2 * c + 1, n), sv("y2", 2 * c + 1, 2 * c + 2, n), ALU.add,
                   "y2_summed")
                dve.wait_ge(S("yrms_ready"), c + 1)
                do(dve.reciprocal(sv("rs", c, c + 1, n), sv("rs", c, c + 1, n)))
                for i in range(2):
                    cols = slice(i * 512, (i + 1) * 512)
                    stt(xn[0:n, c, cols], PB[2 * (c % 2) + i][0:n, :], sv("rs", c, c + 1, n),
                        G[0:n, c // 2, cols], ALU.mult, ALU.mult)
                    tt(x[0:n, c, cols], x[0:n, c, cols], xn[0:n, c, cols], ALU.add)
                dve.nop().then_inc(S("yo_free"), 1)
                dve.nop().then_inc(S("x1_ready"), 1)
            dve.wait_ge(S("rms_ready"), 2)
            do(dve.reciprocal(sv("rs"), sv("rs")))
            for c in range(NCH):
                n = rows_of[c]
                ts(xn[0:n, c, :], x[0:n, c, :], sv("rs", c, c + 1, n), None, ALU.mult)
            dve.nop().then_inc(S("xn2_ready"), 1)
            modulate("h2t", A2, SH2)
            do(dve.memset(xn[:, 2, :], 0.0))
            for c in range(NCH):
                n = rows_of[c]
                for i in range(2):
                    copy(xn[0:n, c, i * 512:(i + 1) * 512], bank(f"h2r{c}{i}")[0:n, :])
                    free()
            do(dve.memset(vaf[:, 0:480], 0.0))
            for c in range(NCH):
                n = rows_of[c]
                tt(lg[0:n, c, :], bank(f"rt{c}")[0:n, 0:E], br[0:n, :], ALU.add)
                free()
                do(dve.max(sv("top", 8 * c, 8 * c + 8, n), lg[0:n, c, :]))
                ts(sv("gr", c, c + 1, n), sv("top", 8 * c, 8 * c + 1, n), -1.0, None, ALU.mult)
                dve.nop().then_inc(S("top_ready"), 1)
                do(dve.max_index(sv("idx", 8 * c, 8 * c + 8, n).bitcast(U32), sv("top", 8 * c, 8 * c + 8, n), lg[0:n, c, :]))
                copy(sv("idf", 8 * c, 8 * c + 8, n), sv("idx", 8 * c, 8 * c + 8, n).bitcast(U32))
                tt(onehot[0:n, c, :, :], C("iota_e", n).unsqueeze(1).to_broadcast([n, TOPK, E]),
                   sv("idf", 8 * c, 8 * c + 4, n).unsqueeze(2).to_broadcast([n, TOPK, E]), ALU.is_equal)
                do(dve.tensor_reduce(mask[0:n, c, :], onehot[0:n, c, :, :].rearrange("p k e -> p e k"), AX, ALU.add))
            dve.nop().then_inc(S("mask_ready"), 1)
            b = bank("pos")
            tot = b[:, NCH * E:(NCH + 1) * E]
            ts(sv("nb"), tot, float(M), 1.0, ALU.is_gt, ALU.add)
            for i in range(2, (T - 1) // M + 1):
                stt(sv("nb"), tot, float(i * M), sv("nb"), ALU.is_gt, ALU.add)
            do(dve.tensor_tensor_scan(sv("incl"), C("ones")[:, 0:E], sv("nb"), 0.0, ALU.mult, ALU.add))
            do(dve.memset(tab[0:1, :], 0))
            copy(tab[0:1, 1:E + 1], sv("incl", rows=1))
            do(dve.memset(used_tab[0:1, :], 0))
            ts(used_tab[0:1, 1:E], sv("incl", 0, E - 1, 1), -1.0, 12.0, ALU.add, ALU.mult)
            dve.nop().then_inc(S("tab_ready"), 1)
            tt(sv("cmp"), sv("incl"), sv("nb"), ALU.subtract)
            for c in range(NCH):
                n = rows_of[c]
                stt(lg[:, c, :], sv("cmp"), float(M), b[:, c * E:(c + 1) * E], ALU.mult, ALU.add)
                tt(eqt[:, 0:TOPK * E].rearrange("p (k e) -> p k e", k=TOPK), onehot[:, c, :, :],
                   lg[:, c, :].unsqueeze(1).to_broadcast([P, TOPK, E]), ALU.mult)
                do(dve.tensor_reduce(sv("g", 4 * c, 4 * c + 4, n),
                                     eqt[0:n, 0:TOPK * E].rearrange("p (k e) -> p k e", k=TOPK), AX, ALU.add))
            free()
            copy(sv("grel"), sv("g"))
            copy(gint[:, :], sv("g"))
            dve.wait_ge(S("ge_ready"), 3)
            for c in range(NCH):
                n = rows_of[c]
                do(dve.reciprocal(sv("gs", c, c + 1, n), sv("gs", c, c + 1, n)))
                ts(sv("ge", 4 * c, 4 * c + 4, n), sv("ge", 4 * c, 4 * c + 4, n), sv("gs", c, c + 1, n), None, ALU.mult)
            spread_rows("g2")

            iota = C("iota_slot").unsqueeze(1).to_broadcast([P, NCH * TOPK, M])
            eq3 = eqt.rearrange("p (g m) -> p g m", m=M)
            g3 = sv("grel").unsqueeze(2).to_broadcast([P, NCH * TOPK, M])
            eq_sum = eqt.rearrange("p (c k m) -> p c m k", c=NCH, k=TOPK)
            P3 = mo["Pm"].rearrange("p (c m) -> p c m", c=NCH)
            do(dve.tensor_tensor(eq3, iota, g3, ALU.is_equal))
            dve.tensor_reduce(P3, eq_sum, AX, ALU.add).then_inc(S("P_ready"), 1)
            dve.wait_ge(S("P_ready"), 1)
            nblocks = dve.value_load(tab[0:1, E:E + 1], min_val=1, max_val=MAXB)
            with dve.Fori(0, nblocks) as b:
                dve.tensor_scalar(sv("grel"), sv("grel"), float(-M), None, ALU.add).then_inc(S("grel_moved"), 1)
                dve.wait_ge(S("grel_moved"), b + 1)
                dve.tensor_tensor(eq3, iota, g3, ALU.is_equal).then_inc(S("eq_ready"), 1)
                dve.wait_ge(S("eq_ready"), b + 1)
                dve.wait_ge(S("gathered"), b + 1)
                dve.tensor_reduce(P3, eq_sum, AX, ALU.add).then_inc(S("P_ready"), 1)
                dve.wait_ge(S("gu_done"), b + 1)
                dve.wait_ge(S("P_ready"), b + 2)
                dve.tensor_scalar(mo["glu"], PB[0][:, :], LIMIT, None, ALU.min).then_inc(S("glu_ready"), 1)
                dve.tensor_scalar(mo["lin"], PB[1][:, :], LIMIT, -LIMIT, ALU.min, ALU.max).then_inc(S("gu_free"), 1)
                dve.wait_ge(S("glu_ready"), b + 1)
                dve.wait_ge(S("gu_free"), b + 1)
                dve.scalar_tensor_tensor(mo["lin"], mo["lin"], 1.0, mo["glu"], ALU.add, ALU.mult).then_inc(S("lg_ready"), 1)
                dve.wait_ge(S("lg_ready"), b + 1)
                dve.wait_ge(S("sig_ready"), b + 1)
                dve.tensor_tensor(mo["actm"], mo["lin"], mo["sig"], ALU.mult).then_inc(S("act_ready"), 1)
            for c in range(NCH):
                n = rows_of[c]
                for k in range(TOPK):
                    i = c * TOPK + k
                    src = ring[0:n, i * D:(i + 1) * D] if i < 8 else late[0:n, (i - 8) * D:(i - 7) * D]
                    dve.wait_ge(S(f"rows{i}_loaded"), 16)
                    gate = sv("ge", i, i + 1, n)
                    if k == 0:
                        ts(xn[0:n, c, :], src, gate, None, ALU.mult)
                    else:
                        stt(xn[0:n, c, :], src, gate, xn[0:n, c, :], ALU.mult, ALU.add)
                dve.nop().then_inc(S("m_ready"), 1)
                dve.wait_ge(S("rms_ready"), 3 + c)
                do(dve.reciprocal(sv("rs", c, c + 1, n), sv("rs", c, c + 1, n)))
                stt(xn[0:n, c, :], xn[0:n, c, :], sv("rs", c, c + 1, n), G[0:n, c // 2, :], ALU.mult, ALU.mult)
                tt(xn[0:n, c, :], xn[0:n, c, :], x[0:n, c, :], ALU.add)
                dve.nop().then_inc(S("final_ready"), 1)


_INS = ["x_prompt", "x_sample", "cache_k", "cache_v", "state_hgrn", "page_table", "c_prompt", "c_sample",
        "w_mod", "b_mod", "g_pre_mix", "g_post_mix", "g_pre_ffn", "g_post_ffn", "w_in", "hgrn_lb", "g_hgrn",
        "lam_q1", "lam_k1", "lam_q2", "lam_k2", "g_subln", "w_proj_a", "w_proj_b", "w_out",
        "w_router", "b_router", "w_gate_up", "b_gate_up", "w_down", "b_down"]
_OUTS = [(1, TP, D), (NS, 1, D), (1, 1, TP, H, DV), (1, 1, TP, H, DV), (1, 1, H, P, DV),
         (1, NS, 1, H, DV), (1, NS, 1, H, DV), (1, NS, H, P, DV)]


def kernel(**inputs):
    import concourse.bacc as bacc
    from concourse.bass_utils import run_bass_kernel_spmd

    nc = bacc.Bacc("TRN2", target_bir_lowering=False, num_devices=1)
    arrays, aps = {}, {}
    given = {n: np.ascontiguousarray(inputs[n]) for n in _INS}
    given["consts"] = constants()
    for name, v in given.items():
        arrays[f"in_{name}"] = v
        aps[name] = nc.dram_tensor(f"in_{name}", v.shape, mybir.dt.from_np(v.dtype), kind="ExternalInput").ap()
    outs = [nc.dram_tensor(f"out_{i}", s, F32, kind="ExternalOutput").ap() for i, s in enumerate(_OUTS)]
    build(nc, aps, outs)
    r = run_bass_kernel_spmd(nc, [arrays], core_ids=[0])
    return tuple(r.results[0][f"out_{i}"] for i in range(len(_OUTS)))
```
